# Optimizing a Trainium2 kernel written in Bass

```python
import jax, jax.numpy as jnp
from jax import lax
import numpy as np

D_MODEL = 1024
BATCH = 1
SEQ = 256
DEPTH = 1

D_RNN = D_MODEL
N_RNN_BLOCKS = 8
RNN_BLOCK = D_RNN // N_RNN_BLOCKS
RNN_CONV_W = 4
LRU_C = 8.0
D_CONF = D_MODEL
CONF_CONV_W = 31
N_GROUPS = 4
EXPERTS_PER_GROUP = 8
N_EXPERTS = N_GROUPS * EXPERTS_PER_GROUP
TOP_K_IN_GROUP = 2
D_EXPERT = 256
RMS_EPS = 1e-6
LN_EPS = 1e-5

SPLITS = (D_RNN, 2 * D_RNN, 2 * D_RNN + D_CONF, 2 * D_RNN + 2 * D_CONF,
          2 * D_RNN + 2 * D_CONF + D_MODEL)
D_IN_PROJ = 2 * D_RNN + 2 * D_CONF + 2 * D_MODEL

kernel_name = "hawk_conformer_hmoe_block"

def rms_norm(x, g):
    xf = x.astype(jnp.float32)
    y = xf * lax.rsqrt(jnp.mean(xf * xf, axis=-1, keepdims=True) + RMS_EPS)
    return (y * g.astype(jnp.float32)).astype(x.dtype)

def layer_norm(x, g, b):
    xf = x.astype(jnp.float32)
    mu = jnp.mean(xf, axis=-1, keepdims=True)
    var = jnp.mean(jnp.square(xf - mu), axis=-1, keepdims=True)
    y = (xf - mu) * lax.rsqrt(var + LN_EPS)
    return (y * g.astype(jnp.float32) + b.astype(jnp.float32)).astype(x.dtype)

def causal_depthwise_conv(x, w, b):
    k, c = w.shape
    out = lax.conv_general_dilated(
        x, w[:, None, :].astype(x.dtype), window_strides=(1,), padding=[(k - 1, 0)],
        dimension_numbers=("NWC", "WIO", "NWC"), feature_group_count=c)
    return out + b.astype(x.dtype)

def block_diag_linear(x, w, b):
    bsz, s, _ = x.shape
    xh = x.reshape(bsz, s, N_RNN_BLOCKS, RNN_BLOCK)
    y = jnp.einsum("bshi,hij->bshj", xh, w.astype(x.dtype)) + b.astype(x.dtype)
    return y.reshape(bsz, s, N_RNN_BLOCKS * RNN_BLOCK)

def rg_lru(x, w_r, b_r, w_i, b_i, a_param):
    r = jax.nn.sigmoid(block_diag_linear(x, w_r, b_r).astype(jnp.float32))
    i = jax.nn.sigmoid(block_diag_linear(x, w_i, b_i).astype(jnp.float32))
    log_a = LRU_C * r * jax.nn.log_sigmoid(a_param.astype(jnp.float32))
    a = jnp.exp(log_a)
    bx = jnp.sqrt(-jnp.expm1(2.0 * log_a)) * (i * x.astype(jnp.float32))

    def combine(left, right):
        a_l, b_l = left
        a_r, b_r = right
        return a_l * a_r, a_r * b_l + b_r

    _, h = lax.associative_scan(combine, (a, bx), axis=1)
    return h.astype(x.dtype)

def token_mixer(u, w_in, rnn_conv_w, rnn_conv_b, lru_w_r, lru_b_r, lru_w_i, lru_b_i,
                lru_a_param, w_rnn_out, conf_conv_w, conf_conv_b, conf_ln_g, conf_ln_b,
                w_conf_out, w_out):
    z = u @ w_in.astype(u.dtype)
    u_rnn, u_gelu, c_val, c_gate, z_ga, z_gb = jnp.split(z, list(SPLITS), axis=-1)
    h = rg_lru(causal_depthwise_conv(u_rnn, rnn_conv_w, rnn_conv_b),
               lru_w_r, lru_b_r, lru_w_i, lru_b_i, lru_a_param)
    y_a = (h * jax.nn.gelu(u_gelu)) @ w_rnn_out.astype(u.dtype)
    c = c_val * jax.nn.sigmoid(c_gate)
    c = causal_depthwise_conv(c, conf_conv_w, conf_conv_b)
    c = jax.nn.silu(layer_norm(c, conf_ln_g, conf_ln_b))
    y_b = c @ w_conf_out.astype(u.dtype)
    mixed = jax.nn.sigmoid(z_ga) * y_a + jax.nn.sigmoid(z_gb) * y_b
    return mixed @ w_out.astype(u.dtype)

def hierarchical_moe(u, w_group_router, b_group_router, w_expert_router, b_expert_router,
                     w_gate, w_up, w_down):
    bsz, s, d = u.shape
    t = u.reshape(bsz * s, d)
    n_tok = t.shape[0]
    g_logits = (t @ w_group_router.astype(t.dtype)).astype(jnp.float32) + b_group_router.astype(jnp.float32)
    g_probs = jax.nn.softmax(g_logits, axis=-1)
    g_val, g_idx = lax.top_k(g_probs, 1)
    e_logits = (t @ w_expert_router.astype(t.dtype)).astype(jnp.float32) + b_expert_router.astype(jnp.float32)
    e_logits = e_logits.reshape(n_tok, N_GROUPS, EXPERTS_PER_GROUP)
    g_onehot = jax.nn.one_hot(g_idx[:, 0], N_GROUPS, dtype=jnp.float32)
    sel_logits = jnp.einsum("tge,tg->te", e_logits, g_onehot)
    in_probs = jax.nn.softmax(sel_logits, axis=-1)
    e_val, e_idx = lax.top_k(in_probs, TOP_K_IN_GROUP)
    e_val = e_val / jnp.sum(e_val, axis=-1, keepdims=True)
    weights = g_val * e_val
    expert_id = g_idx * EXPERTS_PER_GROUP + e_idx
    combine = jnp.einsum("tk,tke->te", weights,
                         jax.nn.one_hot(expert_id, N_EXPERTS, dtype=jnp.float32)).astype(t.dtype)
    out = jnp.zeros_like(t)
    for e in range(N_EXPERTS):
        hid = jax.nn.silu(t @ w_gate[e].astype(t.dtype)) * (t @ w_up[e].astype(t.dtype))
        out = out + combine[:, e:e + 1] * (hid @ w_down[e].astype(t.dtype))
    return out.reshape(bsz, s, d)

def setup_inputs(seed: int = 0) -> dict:
    key = jax.random.key(seed)
    ks = jax.random.split(key, 24)
    f32 = jnp.float32
    L = DEPTH

    def nrm(k, shape, scale):
        return jax.random.normal(k, shape, f32) * scale

    a0 = jax.random.uniform(ks[6], (L, D_RNN), f32, 0.9, 0.999)
    return {
        "x": jax.random.normal(ks[0], (BATCH, SEQ, D_MODEL), f32),
        "g_mix": 1.0 + nrm(ks[1], (L, D_MODEL), 0.01),
        "w_in": nrm(ks[2], (L, D_MODEL, D_IN_PROJ), D_MODEL ** -0.5),
        "rnn_conv_w": nrm(ks[3], (L, RNN_CONV_W, D_RNN), RNN_CONV_W ** -0.5),
        "rnn_conv_b": nrm(ks[4], (L, D_RNN), 0.01),
        "lru_w_r": nrm(ks[5], (L, N_RNN_BLOCKS, RNN_BLOCK, RNN_BLOCK), RNN_BLOCK ** -0.5),
        "lru_b_r": nrm(ks[7], (L, N_RNN_BLOCKS, RNN_BLOCK), 0.01),
        "lru_w_i": nrm(ks[8], (L, N_RNN_BLOCKS, RNN_BLOCK, RNN_BLOCK), RNN_BLOCK ** -0.5),
        "lru_b_i": nrm(ks[9], (L, N_RNN_BLOCKS, RNN_BLOCK), 0.01),
        "lru_a_param": jnp.log(a0) - jnp.log1p(-a0),
        "w_rnn_out": nrm(ks[10], (L, D_RNN, D_MODEL), D_RNN ** -0.5),
        "conf_conv_w": nrm(ks[11], (L, CONF_CONV_W, D_CONF), CONF_CONV_W ** -0.5),
        "conf_conv_b": nrm(ks[12], (L, D_CONF), 0.01),
        "conf_ln_g": 1.0 + nrm(ks[13], (L, D_CONF), 0.01),
        "conf_ln_b": nrm(ks[14], (L, D_CONF), 0.01),
        "w_conf_out": nrm(ks[15], (L, D_CONF, D_MODEL), D_CONF ** -0.5),
        "w_out": nrm(ks[16], (L, D_MODEL, D_MODEL), D_MODEL ** -0.5),
        "g_ffn": 1.0 + nrm(ks[17], (L, D_MODEL), 0.01),
        "w_group_router": nrm(ks[18], (L, D_MODEL, N_GROUPS), D_MODEL ** -0.5),
        "b_group_router": nrm(ks[19], (L, N_GROUPS), 0.01),
        "w_expert_router": nrm(ks[20], (L, D_MODEL, N_EXPERTS), D_MODEL ** -0.5),
        "b_expert_router": nrm(ks[21], (L, N_EXPERTS), 0.01),
        "w_gate": nrm(ks[22], (L, N_EXPERTS, D_MODEL, D_EXPERT), D_MODEL ** -0.5),
        "w_up": nrm(ks[23], (L, N_EXPERTS, D_MODEL, D_EXPERT), D_MODEL ** -0.5),
        "w_down": nrm(jax.random.fold_in(key, 99), (L, N_EXPERTS, D_EXPERT, D_MODEL), D_EXPERT ** -0.5),
        "g_final": 1.0 + nrm(jax.random.fold_in(key, 100), (D_MODEL,), 0.01),
    }

def reference(x, g_mix, w_in, rnn_conv_w, rnn_conv_b, lru_w_r, lru_b_r, lru_w_i, lru_b_i,
              lru_a_param, w_rnn_out, conf_conv_w, conf_conv_b, conf_ln_g, conf_ln_b,
              w_conf_out, w_out, g_ffn, w_group_router, b_group_router, w_expert_router,
              b_expert_router, w_gate, w_up, w_down, g_final):
    h = x
    for l in range(DEPTH):
        h = h + token_mixer(rms_norm(h, g_mix[l]), w_in[l], rnn_conv_w[l], rnn_conv_b[l],
                            lru_w_r[l], lru_b_r[l], lru_w_i[l], lru_b_i[l], lru_a_param[l],
                            w_rnn_out[l], conf_conv_w[l], conf_conv_b[l], conf_ln_g[l],
                            conf_ln_b[l], w_conf_out[l], w_out[l])
        h = h + hierarchical_moe(rms_norm(h, g_ffn[l]), w_group_router[l], b_group_router[l],
                                 w_expert_router[l], b_expert_router[l], w_gate[l], w_up[l],
                                 w_down[l])
    return rms_norm(h, g_final)


_drawn_inputs = setup_inputs


def setup_inputs(seed=0):
    import zlib

    import numpy as np

    out = dict(_drawn_inputs(seed))
    spreads = {}
    factors = {'g_mix': 12.03,
     'rnn_conv_b': 8.801,
     'lru_b_r': 36.98,
     'lru_b_i': 29.551,
     'conf_ln_g': 200.0,
     'conf_ln_b': 200.0,
     'b_group_router': 21.568,
     'b_expert_router': 64.0,
     'g_final': 181.31,
     'conf_conv_b': 8.0,
     'g_ffn': 8.0}
    for name, (base, spread) in spreads.items():
        noise = np.random.default_rng([zlib.crc32(name.encode()), seed]).standard_normal(out[name].shape)
        drawn = base * np.exp(spread * noise) if base else spread * noise
        out[name] = __import__('jax').numpy.asarray(drawn.astype(out[name].dtype))
    for name, factor in factors.items():
        out[name] = (out[name] * factor).astype(out[name].dtype)
    return out
```

```python
from contextlib import ExitStack

import concourse.bass as bass
from concourse import mybir

F32 = mybir.dt.float32
F32R = mybir.dt.float32r
BF16 = mybir.dt.bfloat16
I32 = mybir.dt.int32
ALU = mybir.AluOpType
ACT = mybir.ActivationFunctionType
AX = mybir.AxisListType.X

P = 128
T = 256
TC = T // P
D = 1024
KC = D // P
CONVW = 31
RNNW = 4
LRU_C = 8.0
RMS_EPS = 1e-6
LN_EPS = 1e-5
NG = 4
NE = 32
PER_GROUP = NE // NG
FE = 256
FC = FE // P
SLOTS = 64
QUAD = 4
NQ = NE // QUAD
PANEL = 2048
PN = PANEL // KC
SEG = D // PN
NMIX = 9 * SEG
EXSLOTS = 3 * QUAD

R_GMIX, R_RCB, R_RCW, R_BR, R_BI, R_A, R_CCB, R_LNG, R_LNB, R_GFFN, R_CCW = 0, 1, 2, 6, 7, 8, 9, 10, 11, 12, 13
NROW = R_CCW + CONVW


def bcast(ap, axis, n):
    shape = list(ap.shape)
    shape[axis] = n
    return ap.broadcast_to(shape)


def build(nc, x, g_mix, w_in, rnn_conv_w, rnn_conv_b, lru_w_r, lru_b_r, lru_w_i, lru_b_i, lru_a_param,
          w_rnn_out, conf_conv_w, conf_conv_b, conf_ln_g, conf_ln_b, w_conf_out, w_out, g_ffn,
          w_group_router, b_group_router, w_expert_router, b_expert_router, w_gate, w_up, w_down,
          g_final, out):
    stack = ExitStack()
    mixer_mem = ExitStack()

    def sb(name, shape, dt=F32, where=None):
        return (where or stack).enter_context(nc.sbuf_tensor(name, shape, dt))

    def sem(name):
        return stack.enter_context(nc.semaphore(name))

    with stack:
        ring = sb("ring", [P, EXSLOTS, PANEL])
        hres = sb("hres", [P, TC, D])
        actT = sb("actT", [P, KC, T])
        par = sb("par", [P, KC, NROW])
        ident = sb("ident", [P, P])
        tri = sb("tri", [P, P])
        ones = sb("ones", [P, P])
        wrt = sb("wrt", [P, KC, NG + NE])
        brt = sb("brt", [P, NG + NE])
        stat = sb("stat", [P, 16])
        rounds = sb("rounds", [P, 1], I32)
        iota_s = sb("iota_s", [P, SLOTS])
        desc = sb("desc", [P, NE])
        slot_no = sb("slot_no", [P, 1])
        pair_row = sb("pair_row", [QUAD, 2, P], BF16)
        mixw = sb("mixw", [P, 2, PANEL], F32, mixer_mem)
        bufA = sb("bufA", [P, KC, T + RNNW - 1], F32, mixer_mem)
        cpad = sb("cpad", [P, KC, T + CONVW - 1], F32, mixer_mem)
        bufB = sb("bufB", [P, KC, T], F32, mixer_mem)
        bufC = sb("bufC", [P, KC, T], F32, mixer_mem)
        bufD = sb("bufD", [P, KC, T], F32, mixer_mem)
        bufG = sb("bufG", [P, KC, T], F32, mixer_mem)
        gateA = sb("gateA", [P, KC, T], F32, mixer_mem)
        gateB = sb("gateB", [P, KC, T], F32, mixer_mem)
        vecs = bufB[0:NROW, 0:4, :].rearrange("p a b -> p (a b)")
        xn = bufD[:, :, :].rearrange("p (t a) b -> p t (a b)", t=TC)
        lruw = gateB[:, :, :].rearrange("p (w a) (h j) -> p w (a h) j", w=2, h=2)
        lsc = sb("lsc", [P, 8, KC], F32, mixer_mem)
        cacc = sb("cacc", [P, 2, T], F32, mixer_mem)
        lnw = sb("lnw", [P, 3, T], F32, mixer_mem)
        mixer_mem.close()
        moe_mem = stack
        xslot = sb("xslot", [P, KC, QUAD * SLOTS], F32, moe_mem)
        hn_hi = sb("hn_hi", [P, TC, D], F32R, moe_mem)
        hn_lo = sb("hn_lo", [P, TC, D], F32R, moe_mem)
        sel = sb("sel", [P, TC, QUAD * SLOTS], F32R, moe_mem)
        selT = sb("selT", [P, 2, T], F32R, moe_mem)
        y_hi = sb("y_hi", [P, 2, D], F32R, moe_mem)
        y_lo = sb("y_lo", [P, 2, D], F32R, moe_mem)
        sgate = sb("sgate", [P, FE], F32, moe_mem)
        hid = sb("hid", [P, FE], F32, moe_mem)
        hidT = sb("hidT", [P, FC, P], F32, moe_mem)
        logit = sb("logit", [P, TC, NG + NE], F32, moe_mem)
        rt = sb("rt", [P, 12, TC, NE], F32, moe_mem)
        comb_hl = sb("comb_hl", [P, TC, NE, 2], F32R, moe_mem)
        rank = sb("rank", [P, TC, NE + QUAD], F32, moe_mem)
        rank_q = sb("rank_q", [QUAD, NQ, T], BF16, moe_mem)
        wslot = sb("wslot", [P, 2], F32, moe_mem)
        zeros = sb("zeros", [P, D], F32, moe_mem)
        gfin = sb("gfin", [P, D], F32, moe_mem)
        ps = stack.enter_context(nc.psum_tensor("ps", [P, 8, 512], F32))

        x_in = sem("x_in")
        vec_in = sem("vec_in")
        lruw_in = sem("lruw_in")
        router_in = sem("router_in")
        gfin_in = sem("gfin_in")
        mixw_full = [sem(f"mixw_full{i}") for i in range(2)]
        ex_full = [sem(f"ex_full{i}") for i in range(EXSLOTS)]
        out_done = sem("out_done")
        gp_step = sem("gp_step")
        dve_step = sem("dve_step")
        act_step = sem("act_step")
        dve_xn = sem("dve_xn")
        pe_par = sem("pe_par")
        par_ready = sem("par_ready")
        act_ssq = sem("act_ssq")
        dve_var = sem("dve_var")
        act_std = sem("act_std")
        act_lexp = sem("act_lexp")
        dve_labs = sem("dve_labs")
        dve_lsc = sem("dve_lsc")
        pe_chunk = sem("pe_chunk")
        act_evac = sem("act_evac")
        dve_conv4 = sem("dve_conv4")
        pe_lru = sem("pe_lru")
        act_lru = sem("act_lru")
        dve_lru = sem("dve_lru")
        dve_cmul = sem("dve_cmul")
        dve_conv = sem("dve_conv")
        pe_sum = sem("pe_sum")
        dve_cent = sem("dve_cent")
        act_sq = sem("act_sq")
        dve_norm = sem("dve_norm")
        act_silu = sem("act_silu")
        dve_yb = sem("dve_yb")
        pe_wout = sem("pe_wout")
        dve_h = sem("dve_h")
        pe_hT = sem("pe_hT")
        act_hT = sem("act_hT")
        dve_gw = sem("dve_gw")
        pe_logit = sem("pe_logit")
        dve_rstd2 = sem("dve_rstd2")
        act_hn = sem("act_hn")
        dve_hn = sem("dve_hn")
        dve_route = sem("dve_route")
        act_rexp = sem("act_rexp")
        pe_rank = sem("pe_rank")
        dve_mask = sem("dve_mask")
        dve_rank = sem("dve_rank")
        pe_rankT = sem("pe_rankT")
        dve_rankT = sem("dve_rankT")
        rounds_ready = sem("rounds_ready")
        moe_init = sem("moe_init")
        dve_sel = sem("dve_sel")
        pe_gather = sem("pe_gather")
        act_xslot = sem("act_xslot")
        pe_bc = sem("pe_bc")
        dve_selT = sem("dve_selT")
        pe_gu = sem("pe_gu")
        act_sg = sem("act_sg")
        dve_hid = sem("dve_hid")
        pe_ws = sem("pe_ws")
        dve_ws = sem("dve_ws")
        pe_hidT = sem("pe_hidT")
        act_hidT = sem("act_hidT")
        pe_down = sem("pe_down")
        act_yhi = sem("act_yhi")
        dve_ylo = sem("dve_ylo")
        pe_acc = sem("pe_acc")
        dve_fin = sem("dve_fin")
        act_fssq = sem("act_fssq")
        act_fstd = sem("act_fstd")
        dve_out = sem("dve_out")

        x_v = x.rearrange("b (t p) d -> p (b t) d", p=P)
        out_v = out.rearrange("b (t p) d -> p (b t) d", p=P)

        def rows_by_chunk(w):
            return w.rearrange("(k p) n -> p k n", p=P)

        win_v = rows_by_chunk(w_in[0])
        tail_v = [rows_by_chunk(w[0]) for w in (w_rnn_out, w_conf_out, w_out)]
        SEG_RNN, SEG_GELU, SEG_CVAL, SEG_CGATE, SEG_GA, SEG_GB = range(6)

        def slot_kn(t, s):
            return t[:, s, :].rearrange("p (k n) -> p k n", k=KC)

        block = stack.enter_context(nc.Block())

        @block.sync
        def _(sp):
            sp.dma_start(hres[:, :, :], x_v).then_inc(x_in, 16)

            def expert_panels(q, pair):
                for j in range(2):
                    e = q * QUAD + (2 * pair + j)
                    yield 6 * pair + 2 * j, w_gate, e
                    yield 6 * pair + 2 * j + 1, w_up, e
                for j in range(2):
                    yield 6 * pair + 4 + j, w_down, q * QUAD + (2 * pair + j)

            def load_expert(s, w, e):
                if w is w_down:
                    src = w[0, bass.ds(e, 1), :, :].rearrange("a (f p) n -> p (a f) n", p=P)
                    dst = ring[:, s, :].rearrange("p (f n) -> p f n", f=FC)
                else:
                    src = w[0, bass.ds(e, 1), :, :].rearrange("a (k p) n -> p (a k) n", p=P)
                    dst = slot_kn(ring, s)
                sp.dma_start(dst, src).then_inc(ex_full[s], 16)

            first = [p for pair in range(2) for p in expert_panels(0, pair)]
            order = [(seg, p) for seg in (SEG_RNN,) for p in range(SEG)]
            order += [(seg, p) for p in range(SEG) for seg in (SEG_CVAL, SEG_CGATE)]
            order += [(seg, p) for seg in (SEG_GELU, SEG_GA, SEG_GB, 6, 7, 8) for p in range(SEG)]
            for n in range(NMIX):
                if n >= 2:
                    if n < 8 * SEG + 2:
                        sp.wait_ge(pe_chunk, KC + 2 * (n - 1))
                    else:
                        sp.wait_ge(pe_wout, 2 * (n - 1 - 8 * SEG))
                seg, p = order[n]
                if seg < 6:
                    src = win_v[:, :, seg * D + p * PN: seg * D + (p + 1) * PN]
                else:
                    src = tail_v[seg - 6][:, :, p * PN:(p + 1) * PN]
                sp.dma_start(slot_kn(mixw, n % 2), src).then_inc(mixw_full[n % 2], 16)
                if n >= 4 and n % 2 == 0 and first:
                    load_expert(*first.pop(0))
            while first:
                load_expert(*first.pop(0))
            sp.wait_ge(rounds_ready, 1)
            n_rounds = nc.values_load(rounds[0:1, 0:1], engines=[mybir.EngineType.SP], min_val=1, max_val=4)
            with sp.Fori(1, n_rounds * NQ) as g:
                q = g % NQ
                for pair in range(2):
                    for k, (s, w, e) in enumerate(expert_panels(q, pair)):
                        if k == 0:
                            sp.wait_ge(pe_gu, (g - 1) * 2 + (pair + 1))
                        if k == 4:
                            sp.wait_ge(pe_down, (g - 1) * 2 + (pair + 1))
                        load_expert(s, w, e)
            for tc in range(TC):
                sp.wait_ge(dve_out, tc + 1)
                sp.dma_start(out_v[:, tc, :], hres[:, tc, :]).then_inc(out_done, 16)
            sp.wait_ge(out_done, 16 * TC)

        @block.gpsimd
        def _(gp):
            n = [0]

            def link(ins):
                n[0] += 1
                ins.then_inc(gp_step, 1)
                gp.wait_ge(gp_step, n[0])

            link(gp.memset(ident[:, :], 0.0))
            link(gp.memset(ones[:, :], 1.0))
            link(gp.affine_select(out=ident[:, :], in_=ident[:, :], compare_op=ALU.not_equal, fill=1.0, base=0,
                                  pattern=[[-1, P]], channel_multiplier=1))
            link(gp.affine_select(out=tri[:, :], in_=ones[:, :], compare_op=ALU.is_gt, fill=0.0, base=0,
                                  pattern=[[1, P]], channel_multiplier=-1))
            link(gp.memset(bufA[:, :, 0:RNNW - 1], 0.0))
            link(gp.memset(cpad[:, :, 0:CONVW - 1], 0.0))
            link(gp.iota(iota_s[:, :], pattern=[[1, SLOTS]], base=1, channel_multiplier=0,
                         allow_small_or_imprecise_dtypes=True))
            link(gp.iota(desc[:, :], pattern=[[-1, NE]], base=NE, channel_multiplier=0,
                         allow_small_or_imprecise_dtypes=True))
            for half in (slice(0, SLOTS), slice(SLOTS, P)):
                link(gp.iota(slot_no[half, :], pattern=[[0, 1]], base=1, channel_multiplier=1,
                             allow_small_or_imprecise_dtypes=True))
            link(gp.memset(pair_row[:, :, :], 0.0))
            link(gp.affine_select(out=pair_row[:, :, :].rearrange("q a (b s) -> q (a b) s", b=2),
                                  in_=pair_row[:, :, :].rearrange("q a (b s) -> q (a b) s", b=2),
                                  compare_op=ALU.not_equal, fill=1.0, base=0,
                                  pattern=[[-1, QUAD], [0, SLOTS]], channel_multiplier=1))

        @block.scalar
        def _(act):
            rows = [(R_GMIX, g_mix), (R_RCB, rnn_conv_b), (R_RCW, rnn_conv_w[0]),
                    (R_BR, lru_b_r.rearrange("l h j -> l (h j)")),
                    (R_BI, lru_b_i.rearrange("l h j -> l (h j)")), (R_A, lru_a_param),
                    (R_CCB, conf_conv_b), (R_LNG, conf_ln_g), (R_LNB, conf_ln_b), (R_GFFN, g_ffn),
                    (R_CCW, conf_conv_w[0])]
            for r, v in rows:
                act.dma_start(vecs[r:r + v.shape[0], :], v).then_inc(vec_in, 16)
            act.dma_start(lruw[:, 0, :, :], lru_w_r[0].rearrange("h i j -> i h j")).then_inc(lruw_in, 16)
            act.dma_start(lruw[:, 1, :, :], lru_w_i[0].rearrange("h i j -> i h j")).then_inc(lruw_in, 16)
            act.dma_start(wrt[:, :, 0:NG], rows_by_chunk(w_group_router[0])).then_inc(router_in, 16)
            act.dma_start(wrt[:, :, NG:], rows_by_chunk(w_expert_router[0])).then_inc(router_in, 16)
            act.dma_start(brt[:, 0:NG], bcast(b_group_router, 0, P)).then_inc(router_in, 16)
            act.dma_start(brt[:, NG:], bcast(b_expert_router, 0, P)).then_inc(router_in, 16)

            act.wait_ge(x_in, 16)
            for tc in range(TC):
                if tc:
                    act.wait_ge(act_ssq, tc)
                act.activation(gateA[:, 0:4, :].rearrange("p a b -> p (a b)"), hres[:, tc, :], ACT.Square,
                               accum_out=stat[:, tc:tc + 1]).then_inc(act_ssq, 1)
            act.wait_ge(dve_var, 1)
            act.activation(stat[:, 4:6], stat[:, 2:4], ACT.Sqrt).then_inc(act_std, 1)
            act.wait_ge(dve_labs, 1)
            act.activation(lsc[:, 1, :], lsc[:, 0, :], ACT.Exp, scale=-1.0).then_inc(act_lexp, 1)
            for c in range(KC):
                act.wait_ge(pe_chunk, c + 1)
                act.activation(actT[:, c, :], ps[:, c % 4, 0:T], ACT.Identity,
                               scale=par[:, c, R_GMIX:R_GMIX + 1]).then_inc(act_evac, 1)

            def take_segment(seg, func, dst, before=None):
                base = KC + KC * seg
                with act.Fori(0, KC // 4) as i:
                    for b in range(4):
                        if before:
                            before(i * 4 + b)
                        act.wait_ge(pe_chunk, i * 4 + (base + b + 1))
                        act.activation(dst(i * 4 + b), ps[:, b, 0:T], func).then_inc(act_evac, 1)

            take_segment(0, ACT.Identity,
                         lambda c: bufA[:, bass.ds(c, 1), RNNW - 1:].rearrange("p a b -> p (a b)"))

            def take_conformer(lo, hi):
                with act.Fori(lo, hi) as i:
                    for b in range(4):
                        act.wait_ge(pe_chunk, i * 4 + (2 * KC + b + 1))
                        c = bass.ds(i * 2 + b % 2, 1)
                        d = cpad[:, c, CONVW - 1:] if b < 2 else gateA[:, c, :]
                        act.activation(d.rearrange("p a b -> p (a b)"), ps[:, b, 0:T],
                                       ACT.Identity if b < 2 else ACT.Sigmoid).then_inc(act_evac, 1)

            take_conformer(0, 2)
            for m in range(2 * KC):
                c, w = m // 2, m % 2
                act.wait_ge(pe_lru, m + 1)
                row = (R_BR, R_BI)[w]
                act.activation((bufC, bufD)[w][:, c, :], ps[:, 4 + m % 4, 0:T], ACT.Sigmoid,
                               bias=par[:, c, row:row + 1]).then_inc(act_lru, 1)
            act.wait_ge(dve_lsc, 1)
            act.wait_ge(act_lru, 2 * KC)
            act.wait_ge(dve_conv4, KC)
            for c in range(KC):
                act.activation(bufA[:, c, 0:T], bufC[:, c, :], ACT.Tanh, scale=lsc[:, 7, c:c + 1]
                               ).then_inc(act_lru, 1)
            for c in range(KC):
                act.wait_ge(act_lru, 2 * KC + c + 1)
                act.activation(bufC[:, c, :], bufC[:, c, :], ACT.Exp, scale=lsc[:, 7, c:c + 1]
                               ).then_inc(act_lru, 1)
            take_conformer(2, 4)
            take_segment(3, ACT.Gelu_apprx_tanh,
                         lambda c: bufG[:, bass.ds(c, 1), :].rearrange("p a b -> p (a b)"))
            act.wait_ge(dve_lru, 2)
            act.activation(bufA[:, :, 0:T], bufB[:, :, :], ACT.Sqrt, scale=-1.0).then_inc(act_lru, 1)
            take_segment(4, ACT.Sigmoid,
                         lambda c: gateA[:, bass.ds(c, 1), :].rearrange("p a b -> p (a b)"),
                         before=lambda c: act.wait_ge(dve_cmul, c + 1))
            take_segment(5, ACT.Sigmoid,
                         lambda c: gateB[:, bass.ds(c, 1), :].rearrange("p a b -> p (a b)"))
            act.wait_ge(dve_lru, 3)

            def take_ya(chunks):
                for c in chunks:
                    act.wait_ge(pe_chunk, KC + 6 * KC + c + 1)
                    act.activation(bufA[:, c, 0:T], ps[:, c % 4, 0:T], ACT.Identity).then_inc(act_evac, 1)

            take_ya(range(6))
            act.wait_ge(dve_cent, 1)
            act.activation(bufB[:, :, :], bufC[:, :, :], ACT.Square).then_inc(act_sq, 1)
            act.wait_ge(dve_cent, 2)
            act.activation(lnw[:, 2, :], lnw[:, 1, :], ACT.Sqrt).then_inc(act_sq, 1)
            take_ya(range(6, KC))
            act.wait_ge(dve_norm, 1)
            for c in range(KC):
                act.activation(bufD[:, c, :], bufC[:, c, :], ACT.Silu, scale=par[:, c, R_LNG:R_LNG + 1],
                               bias=par[:, c, R_LNB:R_LNB + 1]).then_inc(act_silu, 1)

            for c in range(KC):
                act.wait_ge(pe_hT, c + 1)
                act.activation(actT[:, c, :], ps[:, c % 2, 0:T], ACT.Identity).then_inc(act_hT, 1)
            act.wait_ge(dve_h, 2 * SEG)
            for tc in range(TC):
                if tc:
                    act.wait_ge(act_ssq, TC + tc)
                act.activation(bufC[:, 0:4, :].rearrange("p a b -> p (a b)"), hres[:, tc, :], ACT.Square,
                               accum_out=stat[:, tc:tc + 1]).then_inc(act_ssq, 1)
            act.wait_ge(dve_var, 2)
            act.activation(stat[:, 4:6], stat[:, 2:4], ACT.Sqrt).then_inc(act_std, 1)
            act.wait_ge(dve_route, 1)
            act.activation(rt[:, 1, :, 0:NG], rt[:, 0, :, 0:NG], ACT.Exp).then_inc(act_rexp, 1)
            act.wait_ge(dve_route, 2)
            act.activation(stat[:, 2:4], stat[:, 8:10], ACT.Exp).then_inc(act_rexp, 1)
            act.wait_ge(dve_rstd2, 1)
            for tc in range(TC):
                act.activation(hn_hi[:, tc, :], hres[:, tc, :], ACT.Copy, scale=stat[:, 6 + tc:7 + tc]
                               ).then_inc(act_hn, 1)
            act.dma_start(gfin[:, :], bcast(g_final.rearrange("(a d) -> a d", a=1), 0, P)).then_inc(gfin_in, 16)

            act.wait_ge(rounds_ready, 1)
            n_rounds = nc.values_load(rounds[0:1, 0:1], engines=[mybir.EngineType.Activation],
                                      min_val=1, max_val=4)
            with act.Fori(0, n_rounds * NQ) as g:
                for c in range(KC):
                    act.wait_ge(pe_gather, g * KC + (c + 1))
                    act.activation(xslot[:, c, :], ps[:, 4 + c % 2, 0:T], ACT.Copy,
                                   scale=par[:, c, R_GFFN:R_GFFN + 1]).then_inc(act_xslot, 1)
                for pair in range(2):
                    act.wait_ge(pe_gu, g * 2 + (pair + 1))
                    act.activation(sgate[:, :], ps[:, 4, 0:FE], ACT.Silu).then_inc(act_sg, 1)
                    act.wait_ge(pe_hidT, g * 2 + (pair + 1))
                    act.activation(hidT[:, :, :].rearrange("p a b -> p (a b)"), ps[:, 4, 0:FE], ACT.Copy
                                   ).then_inc(act_hidT, 1)
                    act.wait_ge(pe_down, g * 2 + (pair + 1))
                    act.wait_ge(dve_ws, g * 4 + (2 * pair + 2))
                    act.activation(y_hi[:, pair, :], ps[:, 6:8, :].rearrange("p a b -> p (a b)"), ACT.Copy,
                                   scale=wslot[:, pair:pair + 1]).then_inc(act_yhi, 1)
            for tc in range(TC):
                act.wait_ge(dve_fin, tc + 1)
                if tc:
                    act.wait_ge(act_fssq, tc)
                act.activation(zeros[:, :], hres[:, tc, :], ACT.Square, accum_out=stat[:, tc:tc + 1]
                               ).then_inc(act_fssq, 1)
            act.wait_ge(dve_fin, TC + 1)
            act.activation(stat[:, 4:6], stat[:, 2:4], ACT.Sqrt).then_inc(act_fstd, 1)

        @block.vector
        def _(v):
            n = [0]

            def step(ins):
                n[0] += 1
                ins.then_inc(dve_step, 1)
                return n[0]

            def link(ins):
                v.wait_ge(dve_step, step(ins))

            v.wait_ge(act_ssq, TC)
            v.tensor_scalar(stat[:, 2:4], stat[:, 0:2], 1.0 / D, RMS_EPS, ALU.mult, ALU.add
                            ).then_inc(dve_var, 1)
            v.wait_ge(act_std, 1)
            link(v.reciprocal(stat[:, 6:8], stat[:, 4:6]))
            for tc in range(TC):
                v.tensor_scalar(xn[:, tc, :], hres[:, tc, :], stat[:, 6 + tc:7 + tc], None, ALU.mult
                                ).then_inc(dve_xn, 1)
            v.wait_ge(pe_par, 1)
            v.tensor_copy(par[:, :, :].rearrange("p k r -> p (k r)"), ps[:, 7, 0:KC * NROW]).then_inc(par_ready, 1)
            v.wait_ge(par_ready, 1)
            a_par = par[:, :, R_A:R_A + 1].rearrange("p k r -> p (k r)")
            link(v.tensor_scalar(lsc[:, 2, :], a_par, -1.0, None, ALU.mult))
            v.tensor_tensor(lsc[:, 0, :], lsc[:, 2, :], a_par, ALU.max).then_inc(dve_labs, 1)
            v.wait_ge(act_lexp, 1)
            link(v.tensor_scalar(lsc[:, 2, :], lsc[:, 1, :], 2.0, None, ALU.add))
            link(v.reciprocal(lsc[:, 3, :], lsc[:, 2, :]))
            link(v.tensor_tensor(lsc[:, 4, :], lsc[:, 1, :], lsc[:, 3, :], ALU.mult))
            link(v.tensor_tensor(lsc[:, 5, :], lsc[:, 4, :], lsc[:, 4, :], ALU.mult))
            link(v.tensor_scalar(lsc[:, 6, :], lsc[:, 5, :], 1.0 / 19, None, ALU.mult))
            for odd in (17, 15, 13, 11, 9, 7, 5, 3):
                link(v.scalar_tensor_tensor(out=lsc[:, 6, :], in0=lsc[:, 6, :], scalar=1.0 / odd,
                                            in1=lsc[:, 5, :], op0=ALU.add, op1=ALU.mult))
            link(v.scalar_tensor_tensor(out=lsc[:, 6, :], in0=lsc[:, 6, :], scalar=1.0,
                                        in1=lsc[:, 4, :], op0=ALU.add, op1=ALU.mult))
            link(v.tensor_scalar(lsc[:, 3, :], a_par, 0.0, LRU_C, ALU.min, ALU.mult))
            v.scalar_tensor_tensor(out=lsc[:, 7, :], in0=lsc[:, 6, :], scalar=-2.0 * LRU_C,
                                   in1=lsc[:, 3, :], op0=ALU.mult, op1=ALU.add).then_inc(dve_lsc, 1)
            v.wait_ge(router_in, 64)
            for c in range(KC):
                v.tensor_scalar(wrt[:, c, :], wrt[:, c, :], par[:, c, R_GFFN:R_GFFN + 1], None, ALU.mult
                                ).then_inc(dve_gw, 1)

            def conv(lo, hi, src, acc, dst, taps, w_row, b_row, before, done):
                per = 2 * (taps - 1)
                base = n[0] - lo * per
                with v.Fori(lo, hi) as i:
                    before(i)
                    for k in range(taps):
                        for j in range(2):
                            c = bass.ds(i * 2 + j, 1)
                            s = src[:, c, k:k + T].rearrange("p a b -> p (a b)")
                            a, d = (x(c, j).rearrange("p a b -> p (a b)") for x in (acc, dst))
                            w = par[:, c, w_row + k:w_row + k + 1].rearrange("p a b -> p (a b)")
                            if k == 0:
                                b = par[:, c, b_row:b_row + 1].rearrange("p a b -> p (a b)")
                                ins = v.tensor_scalar(a, s, w, b, ALU.mult, ALU.add)
                            else:
                                v.wait_ge(dve_step, i * per + (base + 2 * (k - 1) + j + 1))
                                ins = v.scalar_tensor_tensor(out=d if k == taps - 1 else a, in0=s, scalar=w,
                                                             in1=a, op0=ALU.mult, op1=ALU.add)
                            ins.then_inc(done if k == taps - 1 else dve_step, 1)
                n[0] += per * (hi - lo)

            def gated(i):
                v.wait_ge(act_evac, i * 4 + (2 * KC + 4))
                for j in range(2):
                    cc = bass.ds(i * 2 + j, 1)
                    c = cpad[:, cc, CONVW - 1:].rearrange("p a b -> p (a b)")
                    v.tensor_tensor(c, c, gateA[:, cc, :].rearrange("p a b -> p (a b)"), ALU.mult
                                    ).then_inc(dve_cmul, 1)
                v.wait_ge(dve_cmul, i * 2 + 2)

            def conformer_conv(lo, hi):
                conv(lo, hi, cpad, lambda c, j: cacc[:, j:j + 1, :], lambda c, j: cpad[:, c, CONVW - 1:],
                     CONVW, R_CCW, R_CCB, gated, dve_conv)

            v.wait_ge(gp_step, 12)
            conv(0, KC // 2, bufA, lambda c, j: bufB[:, c, :], lambda c, j: bufB[:, c, :], RNNW, R_RCW, R_RCB,
                 lambda i: v.wait_ge(act_evac, i * 2 + (KC + 2)), dve_conv4)
            conformer_conv(0, 1)
            v.wait_ge(act_lru, 2 * KC)
            v.wait_ge(dve_conv4, KC)
            link(v.tensor_tensor(bufD[:, :, :], bufD[:, :, :], bufB[:, :, :], ALU.mult))
            v.wait_ge(act_lru, 4 * KC)
            v.tensor_tensor(bufB[:, :, :], bufC[:, :, :], bufC[:, :, :], ALU.mult).then_inc(dve_lru, 1)
            v.wait_ge(dve_lru, 1)
            v.scalar_tensor_tensor(out=bufB[:, :, :], in0=bufB[:, :, :], scalar=1.0, in1=bufA[:, :, 0:T],
                                   op0=ALU.add, op1=ALU.mult).then_inc(dve_lru, 1)
            conformer_conv(1, 3)
            v.wait_ge(act_lru, 4 * KC + 1)
            v.tensor_tensor(bufD[:, :, :], bufD[:, :, :], bufA[:, :, 0:T], ALU.mult).then_inc(dve_lru, 1)
            v.wait_ge(dve_lru, 3)
            for c in range(KC):
                last = step(v.tensor_tensor_scan(bufB[:, c, :], bufC[:, c, :], bufD[:, c, :], 0.0,
                                                 ALU.mult, ALU.add))
            v.wait_ge(dve_step, last)
            v.wait_ge(act_evac, 5 * KC)
            v.tensor_tensor(bufG[:, :, :], bufG[:, :, :], bufB[:, :, :], ALU.mult).then_inc(dve_lru, 1)
            conformer_conv(3, 4)
            v.wait_ge(pe_sum, 1)
            v.wait_ge(dve_conv, KC)
            link(v.tensor_scalar(lnw[:, 0, :], ps[:, 4, 0:T], 1.0 / D, None, ALU.mult))
            mean = bcast(lnw[:, 0:1, :], 1, KC)
            v.tensor_tensor(bufC[:, :, :], cpad[:, :, CONVW - 1:], mean, ALU.subtract).then_inc(dve_cent, 1)
            v.wait_ge(pe_sum, 2)
            v.tensor_scalar(lnw[:, 1, :], ps[:, 5, 0:T], 1.0 / D, LN_EPS, ALU.mult, ALU.add).then_inc(dve_cent, 1)
            v.wait_ge(act_sq, 2)
            link(v.reciprocal(lnw[:, 0, :], lnw[:, 2, :]))
            v.tensor_tensor(bufC[:, :, :], bufC[:, :, :], bcast(lnw[:, 0:1, :], 1, KC), ALU.mult
                            ).then_inc(dve_norm, 1)
            v.wait_ge(act_evac, 8 * KC)
            link(v.tensor_tensor(gateA[:, :, :], gateA[:, :, :], bufA[:, :, 0:T], ALU.mult))
            for c in range(KC):
                v.wait_ge(pe_chunk, KC + 7 * KC + c + 1)
                v.tensor_tensor(gateB[:, c, :], gateB[:, c, :], ps[:, c % 4, 0:T], ALU.mult).then_inc(dve_yb, 1)
                v.wait_ge(dve_yb, 2 * c + 1)
                v.tensor_tensor(gateA[:, c, :], gateA[:, c, :], gateB[:, c, :], ALU.add).then_inc(dve_yb, 1)
            for p in range(SEG):
                for tc in range(TC):
                    v.wait_ge(pe_wout, 2 * p + tc + 1)
                    hcol = hres[:, tc, p * PN:(p + 1) * PN]
                    v.tensor_tensor(hcol, hcol, ps[:, 4 + tc, 0:PN], ALU.add).then_inc(dve_h, 1)
            v.wait_ge(act_ssq, 2 * TC)
            v.tensor_scalar(stat[:, 2:4], stat[:, 0:2], 1.0 / D, RMS_EPS, ALU.mult, ALU.add).then_inc(dve_var, 1)
            v.wait_ge(act_std, 2)
            v.reciprocal(stat[:, 6:8], stat[:, 4:6]).then_inc(dve_rstd2, 1)
            v.wait_ge(dve_rstd2, 1)

            def col(k):
                return stat[:, k:k + TC].rearrange("p (t a) -> p t a", a=1)

            v.wait_ge(pe_logit, 1)
            for tc in range(TC):
                last = step(v.scalar_tensor_tensor(out=logit[:, tc, :], in0=ps[:, 2 + tc, 0:NG + NE],
                                                   scalar=stat[:, 6 + tc:7 + tc], in1=brt[:, :],
                                                   op0=ALU.mult, op1=ALU.add))
            v.wait_ge(dve_step, last)
            gl = logit[:, :, 0:NG]
            el = logit[:, :, NG:NG + NE]

            def first_of(dst, src, top, width, tmp):
                link(v.tensor_tensor(rt[:, tmp, :, 0:width], src, bcast(top, 2, width), ALU.is_equal))
                d = bcast(desc[:, 0:width].rearrange("p (a w) -> p a w", a=1), 1, TC)
                link(v.tensor_tensor(rt[:, tmp, :, 0:width], rt[:, tmp, :, 0:width], d, ALU.mult))
                link(v.tensor_reduce(stat[:, 14:16], rt[:, tmp, :, 0:width], AX, ALU.max))
                link(v.tensor_tensor(dst, rt[:, tmp, :, 0:width], bcast(col(14), 2, width), ALU.is_equal))

            link(v.tensor_reduce(stat[:, 12:14], gl, AX, ALU.max))
            v.tensor_tensor(rt[:, 0, :, 0:NG], gl, bcast(col(12), 2, NG), ALU.subtract).then_inc(dve_route, 1)
            first_of(rt[:, 2, :, 0:NG], gl, col(12), NG, 3)
            link(v.tensor_scalar(rt[:, 3, :, 0:NG], rt[:, 2, :, 0:NG], -1.0, 1e30, ALU.add, ALU.mult))
            e4 = rt[:, 4, :, :].rearrange("p t (g e) -> p (t g) e", g=NG)
            for tc in range(TC):
                drop = bcast(rt[:, 3, tc, 0:NG].rearrange("p (g a) -> p g a", a=1), 2, PER_GROUP)
                last = step(v.tensor_tensor(rt[:, 4, tc, :].rearrange("p (g e) -> p g e", g=NG),
                                            logit[:, tc, NG:].rearrange("p (g e) -> p g e", g=NG),
                                            drop, ALU.add))
            v.wait_ge(dve_step, last)
            link(v.tensor_reduce(stat[:, 12:14], rt[:, 4, :, :], AX, ALU.max))
            first_of(rt[:, 5, :, :], rt[:, 4, :, :], col(12), NE, 6)
            link(v.scalar_tensor_tensor(out=rt[:, 7, :, :], in0=rt[:, 5, :, :], scalar=-2e30,
                                        in1=rt[:, 4, :, :], op0=ALU.mult, op1=ALU.add))
            link(v.tensor_reduce(stat[:, 10:12], rt[:, 7, :, :], AX, ALU.max))
            v.tensor_tensor(stat[:, 8:10], stat[:, 10:12], stat[:, 12:14], ALU.subtract).then_inc(dve_route, 1)
            first_of(rt[:, 8, :, :], rt[:, 7, :, :], col(10), NE, 6)
            v.tensor_tensor(rt[:, 9, :, :], rt[:, 5, :, :], rt[:, 8, :, :], ALU.add).then_inc(dve_mask, 1)
            v.wait_ge(act_rexp, 1)
            link(v.tensor_reduce(stat[:, 12:14], rt[:, 1, :, 0:NG], AX, ALU.add))
            v.wait_ge(act_rexp, 2)
            link(v.scalar_tensor_tensor(out=stat[:, 14:16], in0=stat[:, 2:4], scalar=1.0,
                                        in1=stat[:, 12:14], op0=ALU.add, op1=ALU.mult))
            link(v.reciprocal(stat[:, 12:14], stat[:, 14:16]))
            link(v.tensor_tensor(stat[:, 14:16], stat[:, 12:14], stat[:, 2:4], ALU.mult))
            link(v.tensor_tensor(rt[:, 5, :, :], rt[:, 5, :, :], bcast(col(12), 2, NE), ALU.mult))
            link(v.tensor_tensor(rt[:, 8, :, :], rt[:, 8, :, :], bcast(col(14), 2, NE), ALU.mult))
            link(v.tensor_tensor(rt[:, 10, :, :], rt[:, 5, :, :], rt[:, 8, :, :], ALU.add))
            hi = comb_hl[:, :, :, 0:1].rearrange("p t e a -> p t (e a)")
            lo = comb_hl[:, :, :, 1:2].rearrange("p t e a -> p t (e a)")
            link(v.tensor_copy(hi, rt[:, 10, :, :]))
            step(v.tensor_tensor(lo, rt[:, 10, :, :], hi.bitcast(F32), ALU.subtract))
            v.wait_ge(pe_rank, 1)
            for tc in range(TC):
                last = step(v.scalar_tensor_tensor(out=rank[:, tc, 0:NE], in0=ps[:, 6, NE * tc:NE * (tc + 1)],
                                                   scalar=1.0, in1=rt[:, 9, tc, :], op0=ALU.add, op1=ALU.mult))
            v.wait_ge(dve_step, last)
            v.tensor_scalar(rank[:, :, NE:], rank[:, :, 0:QUAD], -float(SLOTS), None, ALU.add
                            ).then_inc(dve_rank, 1)
            link(v.tensor_reduce(stat[:, 12:13], ps[:, 6, 2 * NE:3 * NE], AX, ALU.max))
            link(v.tensor_scalar(stat[:, 13:14], stat[:, 12:13], float(SLOTS), 1.0, ALU.is_gt, ALU.add))
            for k in range(2, T // SLOTS):
                link(v.scalar_tensor_tensor(out=stat[:, 13:14], in0=stat[:, 12:13], scalar=float(k * SLOTS),
                                            in1=stat[:, 13:14], op0=ALU.is_gt, op1=ALU.add))
            v.tensor_copy(rounds[:, :], stat[:, 13:14]).then_inc(rounds_ready, 1)

            def fill_sel(q):
                for tc in range(TC):
                    ins = v.tensor_tensor(
                        sel[:, tc, :].rearrange("p (e s) -> p e s", s=SLOTS),
                        bcast(rank[:, tc, q].rearrange("p (e a) -> p e a", a=1), 2, SLOTS),
                        bcast(iota_s[:, :].rearrange("p (a s) -> p a s", a=1), 1, QUAD), ALU.is_equal)
                return ins

            v.wait_ge(dve_rank, 1)
            fill_sel(slice(0, QUAD)).then_inc(dve_sel, 1)
            v.wait_ge(pe_rankT, 1)
            v.tensor_copy(rank_q[:, :, :].rearrange("e q t -> e (q t)"),
                          ps[0:QUAD, 0:4, :].rearrange("e a b -> e (a b)")).then_inc(dve_rankT, 1)
            for tc in range(TC):
                v.wait_ge(act_hn, tc + 1)
                v.scalar_tensor_tensor(out=hn_lo[:, tc, :], in0=hres[:, tc, :], scalar=stat[:, 6 + tc:7 + tc],
                                       in1=hn_hi[:, tc, :].bitcast(F32), op0=ALU.mult, op1=ALU.subtract
                                       ).then_inc(dve_hn, 1)
            link(v.memset(zeros[:, :], 0.0))
            v.tensor_copy(y_hi[:, 1, :], zeros[:, :]).then_inc(moe_init, 1)
            v.tensor_copy(y_lo[:, 1, :], zeros[:, :]).then_inc(dve_ylo, 1)
            v.tensor_copy(selT[:, 1, :], zeros[:, 0:T]).then_inc(dve_selT, 1)

            v.wait_ge(rounds_ready, 1)
            n_rounds = nc.values_load(rounds[0:1, 0:1], engines=[mybir.EngineType.DVE], min_val=1, max_val=4)
            own = n[0]
            with v.Fori(0, n_rounds) as r:
                with v.Fori(0, NQ) as q:
                    g = r * NQ + q
                    v.wait_ge(pe_bc, g + 1)
                    v.tensor_scalar(selT[:, :, :].rearrange("p a t -> p (a t)"), ps[:, 5, :], slot_no[:, 0:1],
                                    None, ALU.is_equal).then_inc(dve_selT, 1)
                    for pair in range(2):
                        v.wait_ge(pe_ws, g * 2 + (pair + 1))
                        for j in range(2):
                            half = slice(SLOTS * j, SLOTS * (j + 1))
                            v.tensor_reduce(wslot[half, pair:pair + 1], ps[half, 6, 2 * j:2 * j + 2], AX, ALU.add
                                            ).then_inc(dve_ws, 1)
                        v.wait_ge(act_sg, g * 2 + (pair + 1))
                        v.tensor_tensor(hid[:, :], sgate[:, :], ps[:, 4, FE:2 * FE], ALU.mult).then_inc(dve_hid, 1)
                        if pair == 1:
                            fill_sel(bass.ds((q + 1) * QUAD, QUAD)).then_inc(dve_sel, 1)
                        v.wait_ge(act_yhi, g * 2 + (pair + 1))
                        v.wait_ge(dve_ws, g * 4 + (2 * pair + 2))
                        v.scalar_tensor_tensor(out=y_lo[:, pair, :], in0=ps[:, 6:8, :].rearrange("p a b -> p (a b)"),
                                               scalar=wslot[:, pair:pair + 1],
                                               in1=y_hi[:, pair, :].bitcast(F32),
                                               op0=ALU.mult, op1=ALU.subtract).then_inc(dve_ylo, 1)
                v.wait_ge(dve_sel, (r + 1) * NQ + 1)
                v.tensor_scalar(rank[:, :, :], rank[:, :, :], -float(SLOTS), None, ALU.add).then_inc(dve_step, 1)
                v.wait_ge(dve_selT, (r + 1) * NQ + 1)
                v.tensor_scalar(slot_no[:, :], slot_no[:, :], float(SLOTS), None, ALU.add).then_inc(dve_step, 1)
                v.wait_ge(dve_step, r * 2 + (own + 2))
            v.wait_ge(pe_acc, 1)
            for tc in range(TC):
                v.tensor_tensor(hres[:, tc, :], hres[:, tc, :],
                                ps[:, 2 * tc:2 * tc + 2, :].rearrange("p a b -> p (a b)"), ALU.add
                                ).then_inc(dve_fin, 1)
            v.wait_ge(act_fssq, TC)
            v.tensor_scalar(stat[:, 2:4], stat[:, 0:2], 1.0 / D, RMS_EPS, ALU.mult, ALU.add).then_inc(dve_fin, 1)
            v.wait_ge(act_fstd, 1)
            v.reciprocal(stat[:, 6:8], stat[:, 4:6]).then_inc(dve_fin, 1)
            v.wait_ge(dve_fin, TC + 2)
            v.wait_ge(gfin_in, 16)
            for tc in range(TC):
                v.scalar_tensor_tensor(out=hres[:, tc, :], in0=hres[:, tc, :], scalar=stat[:, 6 + tc:7 + tc],
                                       in1=gfin[:, :], op0=ALU.mult, op1=ALU.mult).then_inc(dve_out, 1)

        @block.tensor
        def _(pe):
            pe.wait_ge(gp_step, 4)
            pe.wait_ge(vec_in, 16 * 11)
            for c in range(KC):
                last = pe.transpose(ps[:, 7, c * NROW:(c + 1) * NROW], vecs[:, c * P:(c + 1) * P],
                                    ident[0:NROW, 0:NROW])
            last.then_inc(pe_par, 1)
            pe.wait_ge(par_ready, 1)
            for c in range(KC):
                if c >= 4:
                    pe.wait_ge(act_evac, c - 3)
                for tc in range(TC):
                    if c == 0:
                        pe.wait_ge(dve_xn, tc + 1)
                    last = pe.transpose(ps[:, c % 4, tc * P:(tc + 1) * P], xn[:, tc, c * P:(c + 1) * P],
                                        ident[:, :])
                last.then_inc(pe_chunk, 1)

            def panel_chunks(p, rhs, before):
                w = slot_kn(mixw, p % 2)
                for h in range(2):
                    before(2 * p + h)
                    for k in range(KC):
                        last = pe.matmul(ps[:, (2 * p + h) % 4, 0:T], w[:, k, h * P:(h + 1) * P], rhs[:, k, 0:T],
                                         start=(k == 0), stop=(k == KC - 1))
                    last.then_inc(pe_chunk, 1)

            def w_in_segments(lo, hi):
                with pe.Fori(lo, hi) as s:
                    for p in range(SEG):
                        pe.wait_ge(mixw_full[p % 2], s * (8 * SEG) + 16 * (p // 2 + 1))
                        panel_chunks(p, actT, lambda m: pe.wait_ge(act_evac, s * KC + (KC + m - 3)))

            def mix_panel_here(n):
                pe.wait_ge(mixw_full[n % 2], 16 * (n // 2 + 1))

            pe.wait_ge(act_evac, KC)
            w_in_segments(0, 2)
            pe.wait_ge(lruw_in, 32)
            for m in range(2 * KC):
                c, w = m // 2, m % 2
                if w == 0:
                    pe.wait_ge(dve_conv4, c + 1)
                if m >= 4:
                    pe.wait_ge(act_lru, m - 3)
                pe.matmul(ps[:, 4 + m % 4, 0:T], lruw[:, w, c, :], bufB[:, c, :], start=True, stop=True
                          ).then_inc(pe_lru, 1)
            w_in_segments(2, 6)

            def channel_sums(src, bank):
                for c in range(KC):
                    last = pe.matmul(ps[:, bank, 0:T], ones[:, :], src[:, c, :], start=(c == 0), stop=(c == KC - 1))
                last.then_inc(pe_sum, 1)

            pe.wait_ge(dve_lru, 4)
            for p in range(SEG):
                mix_panel_here(6 * SEG + p)
                panel_chunks(p, bufG, lambda m: pe.wait_ge(act_evac, 7 * KC + m - 3))
                if p == 1:
                    pe.wait_ge(dve_conv, KC)
                    channel_sums(cpad[:, :, CONVW - 1:], 4)
                if p == 2:
                    pe.wait_ge(act_sq, 1)
                    channel_sums(bufB, 5)
            pe.wait_ge(act_silu, KC)

            def yb_bank(m):
                if m < 4:
                    pe.wait_ge(act_evac, 8 * KC + m - 3)
                else:
                    pe.wait_ge(dve_yb, 2 * (m - 3) - 1)
            for p in range(SEG):
                mix_panel_here(7 * SEG + p)
                panel_chunks(p, bufD, yb_bank)
            pe.wait_ge(dve_yb, 2 * KC)

            def h_transposes(p):
                for c in (2 * p, 2 * p + 1):
                    if c >= 2:
                        pe.wait_ge(act_hT, c - 1)
                    for tc in range(TC):
                        pe.wait_ge(dve_h, 2 * p + tc + 1)
                        last = pe.transpose(ps[:, c % 2, tc * P:(tc + 1) * P], hres[:, tc, c * P:(c + 1) * P],
                                            ident[:, :])
                    last.then_inc(pe_hT, 1)

            def logits(p):
                for c in (2 * p, 2 * p + 1):
                    pe.wait_ge(act_hT, c + 1)
                    for tc in range(TC):
                        last = pe.matmul(ps[:, 2 + tc, 0:NG + NE], actT[:, c, tc * P:(tc + 1) * P], wrt[:, c, :],
                                         start=(c == 0), stop=(c == KC - 1))
                return last

            pe.wait_ge(dve_gw, KC)
            for p in range(SEG):
                mix_panel_here(8 * SEG + p)
                w = slot_kn(mixw, p % 2)
                for tc in range(TC):
                    if p:
                        pe.wait_ge(dve_h, 2 * (p - 1) + tc + 1)
                    for k in range(KC):
                        last = pe.matmul(ps[:, 4 + tc, 0:PN], gateA[:, k, tc * P:(tc + 1) * P], w[:, k, :],
                                         start=(k == 0), stop=(k == KC - 1))
                    last.then_inc(pe_wout, 1)
                if p >= 1:
                    h_transposes(p - 1)
                if p >= 2:
                    logits(p - 2)
            h_transposes(SEG - 1)
            logits(SEG - 2)
            logits(SEG - 1).then_inc(pe_logit, 1)
            pe.wait_ge(dve_mask, 1)
            mask = rt[:, 9, :, :]
            pe.matmul(ps[:, 6, 0:NE], tri[:, :], mask[:, 0, :], start=True, stop=True)
            pe.matmul(ps[:, 6, NE:2 * NE], ones[:, :], mask[:, 0, :], start=True, stop=False)
            pe.matmul(ps[:, 6, NE:2 * NE], tri[:, :], mask[:, 1, :], start=False, stop=True)
            pe.matmul(ps[:, 6, 2 * NE:3 * NE], ones[:, :], mask[:, 0, :], start=True, stop=False)
            pe.matmul(ps[:, 6, 2 * NE:3 * NE], ones[:, :], mask[:, 1, :], start=False, stop=True
                      ).then_inc(pe_rank, 1)
            pe.wait_ge(dve_rank, 1)
            for q in range(NQ):
                for tc in range(TC):
                    at = (q % 2) * T + tc * P
                    last = pe.transpose(ps[0:QUAD, q // 2, at:at + P], rank[:, tc, q * QUAD:(q + 1) * QUAD],
                                        ident[:, :])
            last.then_inc(pe_rankT, 1)

            def scatter(pair, start=False, stop=False, parts=(y_hi, y_lo), chunks=range(TC)):
                for tc in chunks:
                    for nn in range(2):
                        for y in parts:
                            last = pe.matmul(ps[:, 2 * tc + nn, :], selT[:, pair, tc * P:(tc + 1) * P],
                                             y[:, pair, nn * 512:(nn + 1) * 512],
                                             start=start, stop=stop and y is y_lo, skip_group_check=True)
                return last

            pe.wait_ge(moe_init, 1)
            pe.wait_ge(dve_ylo, 1)
            pe.wait_ge(dve_selT, 1)
            pe.wait_ge(dve_rankT, 1)
            scatter(1, start=True, parts=(y_hi,))
            pe.wait_ge(dve_hn, TC)
            pe.wait_ge(rounds_ready, 1)
            n_rounds = nc.values_load(rounds[0:1, 0:1], engines=[mybir.EngineType.PE], min_val=1, max_val=4)
            with pe.Fori(0, n_rounds * NQ) as g:
                q = g % NQ
                pe.wait_ge(dve_sel, g + 1)
                pe.wait_ge(dve_selT, g + 1)
                for c in range(KC):
                    if c >= 2:
                        pe.wait_ge(act_xslot, g * KC + (c - 1))
                    for i, (part, tc) in enumerate([(a, b) for a in (hn_hi, hn_lo) for b in range(TC)]):
                        last = pe.matmul(ps[:, 4 + c % 2, 0:T], part[:, tc, c * P:(c + 1) * P],
                                         sel[:, tc, :], start=(i == 0), stop=(i == 2 * TC - 1))
                    last.then_inc(pe_gather, 1)
                pe.wait_ge(dve_ylo, g * 2 + 1)
                scatter(1, chunks=[0])
                pe.wait_ge(act_xslot, g * KC + KC)
                scatter(1, chunks=[1])
                for pair in range(2):
                    last = pe.matmul(ps[:, 5, pair * T:(pair + 1) * T], pair_row[:, pair, :],
                                     rank_q[:, bass.ds(q, 1), :].rearrange("e a t -> e (a t)"),
                                     start=True, stop=True)
                last.then_inc(pe_bc, 1)
                for pair in range(2):
                    for s in range(6 * pair, 6 * pair + 4):
                        pe.wait_ge(ex_full[s], g * 16 + 16)
                    if pair == 1:
                        pe.wait_ge(act_hidT, g * 2 + 1)
                    for k in range(KC):
                        for j in range(2):
                            s = 6 * pair + 2 * j
                            e = 2 * pair + j
                            w = ring[:, s:s + 2, k * FE:(k + 1) * FE]
                            last = pe.matmul(ps[SLOTS * j:SLOTS * (j + 1), 4, :],
                                             xslot[:, k, e * SLOTS:(e + 1) * SLOTS], w,
                                             start=(k == 0), stop=(k == KC - 1), skip_group_check=True)
                    last.then_inc(pe_gu, 1)
                    pe.wait_ge(dve_ylo, g * 2 + (pair + 1))
                    for tc in range(TC):
                        last = pe.matmul(ps[:, 6, 0:4], sel[:, tc, pair * P:(pair + 1) * P],
                                         comb_hl[:, tc, bass.ds(q * QUAD + 2 * pair, 2), :].rearrange("p a b -> p (a b)"),
                                         start=(tc == 0), stop=(tc == TC - 1))
                    last.then_inc(pe_ws, 1)
                    if pair == 1:
                        scatter(0)
                    pe.wait_ge(dve_hid, g * 2 + (pair + 1))
                    for f in range(FC):
                        last = pe.transpose(ps[:, 4, f * P:(f + 1) * P], hid[:, f * P:(f + 1) * P], ident[:, :])
                    last.then_inc(pe_hidT, 1)
                    pe.wait_ge(ex_full[6 * pair + 4], g * 16 + 16)
                    pe.wait_ge(ex_full[6 * pair + 5], g * 16 + 16)
                    pe.wait_ge(act_hidT, g * 2 + (pair + 1))
                    pe.wait_ge(dve_ws, g * 4 + (2 * pair + 2))
                    for nn in range(2):
                        for f in range(FC):
                            for j in range(2):
                                w = ring[:, 6 * pair + 4 + j, :].rearrange("p (f n) -> p f n", f=FC)
                                last = pe.matmul(ps[SLOTS * j:SLOTS * (j + 1), 6 + nn, :],
                                                 hidT[:, f, SLOTS * j:SLOTS * (j + 1)],
                                                 w[:, f, nn * 512:(nn + 1) * 512],
                                                 start=(f == 0), stop=(f == FC - 1), skip_group_check=True)
                    last.then_inc(pe_down, 1)
            pe.wait_ge(dve_ylo, n_rounds * (2 * NQ) + 1)
            scatter(1, stop=True).then_inc(pe_acc, 1)


_INS = ["x", "g_mix", "w_in", "rnn_conv_w", "rnn_conv_b", "lru_w_r", "lru_b_r", "lru_w_i", "lru_b_i",
        "lru_a_param", "w_rnn_out", "conf_conv_w", "conf_conv_b", "conf_ln_g", "conf_ln_b", "w_conf_out",
        "w_out", "g_ffn", "w_group_router", "b_group_router", "w_expert_router", "b_expert_router",
        "w_gate", "w_up", "w_down", "g_final"]


def kernel(**inputs):
    import numpy as np
    import concourse.bacc as bacc
    from concourse.bass_utils import run_bass_kernel_spmd

    nc = bacc.Bacc("TRN2", target_bir_lowering=False, num_devices=1)
    arrays, args = {}, []
    for name in _INS:
        a = np.ascontiguousarray(inputs[name])
        arrays[f"in_{name}"] = a
        args.append(nc.dram_tensor(f"in_{name}", a.shape, mybir.dt.from_np(a.dtype), kind="ExternalInput").ap())
    shape = inputs["x"].shape
    out = nc.dram_tensor("out", shape, F32, kind="ExternalOutput").ap()
    build(nc, *args, out)
    r = run_bass_kernel_spmd(nc, [arrays], core_ids=[0])
    return r.results[0]["out"]
```

```python
from contextlib import ExitStack

import concourse.bass as bass
from concourse import mybir

F32 = mybir.dt.float32
F32R = mybir.dt.float32r
BF16 = mybir.dt.bfloat16
I32 = mybir.dt.int32
ALU = mybir.AluOpType
ACT = mybir.ActivationFunctionType
ENG = mybir.EngineType
AX = mybir.AxisListType.X

P = 128
T = 256
TC = T // P
D = 1024
KC = D // P
CONVW = 31
RNNW = 4
LRU_C = 8.0
RMS_EPS = 1e-6
LN_EPS = 1e-5
NG = 4
NE = 32
PER_GROUP = NE // NG
FE = 256
FC = FE // P
SLOTS = 64
QUAD = 4
NQ = NE // QUAD
PANEL = 2048
PN = PANEL // KC
SEG = D // PN
NMIX = 9 * SEG
EXSLOTS = 3 * QUAD
K_CONF, K_RNN, K_GELU, K_SPLIT, K_WOUT = 0, 2 * SEG, 3 * SEG, 4 * SEG, 8 * SEG
HI_SLOT, MIX_SLOT = SEG, 2 * SEG

R_GMIX, R_RCB, R_RCW, R_BR, R_BI, R_A, R_CCB, R_LNG, R_LNB, R_GFFN, R_CCW = 0, 1, 2, 6, 7, 8, 9, 10, 11, 12, 13
NROW = R_CCW + CONVW


def bcast(ap, axis, n):
    shape = list(ap.shape)
    shape[axis] = n
    return ap.broadcast_to(shape)


def build(nc, x, g_mix, w_in, rnn_conv_w, rnn_conv_b, lru_w_r, lru_b_r, lru_w_i, lru_b_i, lru_a_param,
          w_rnn_out, conf_conv_w, conf_conv_b, conf_ln_g, conf_ln_b, w_conf_out, w_out, g_ffn,
          w_group_router, b_group_router, w_expert_router, b_expert_router, w_gate, w_up, w_down,
          g_final, out):
    stack = ExitStack()
    mixer_mem = ExitStack()

    def sb(name, shape, dt=F32, where=None):
        return (where or stack).enter_context(nc.sbuf_tensor(name, shape, dt))

    def loop(engine, lo, hi):
        return nc.Fori(lo, hi, engines=(engine,), hint_back_edge=True)

    def sem(name):
        return stack.enter_context(nc.semaphore(name))

    with stack:
        with ExitStack() as alias:
            ring = sb("ring", [P, EXSLOTS, PANEL], F32, alias)
        ring_r = sb("ring_r", [P, EXSLOTS, PANEL], F32R)
        hres = sb("hres", [P, TC, D])
        actT = sb("actT", [P, KC, T])
        par = sb("par", [P, KC, NROW])
        ident = sb("ident", [P, P])
        tri = sb("tri", [P, P])
        ones = sb("ones", [P, P])
        wrt = sb("wrt", [P, KC, NG + NE])
        brt = sb("brt", [P, NG + NE])
        stat = sb("stat", [P, 16])
        rounds = sb("rounds", [P, 1], I32)
        iota_s = sb("iota_s", [P, SLOTS])
        desc = sb("desc", [P, NE])
        slot_no = sb("slot_no", [P, 1])
        pair_row = sb("pair_row", [QUAD, 2, P], BF16)
        selT = sb("selT", [P, 2, T], F32R)
        wslot = sb("wslot", [P, 2])
        ssp = sb("ssp", [P, TC, SEG])
        u_hi = sb("u_hi", [P, KC, T], F32R, mixer_mem)
        u_lo = sb("u_lo", [P, KC, T], F32R, mixer_mem)
        MIXER = [("bufA", RNNW - 1), ("cpad", CONVW - 1), ("bufC", 0), ("bufG", 0), ("gateA", 0),
                 ("bufB", 0), ("bufD", 0), ("gateB", 0)]
        with ExitStack() as alias:
            bufA, cpad, bufC, bufG, gateA, bufB, bufD, gateB = (
                sb(name, [P, KC, T + pad], F32, alias) for name, pad in MIXER)
        bufA_r, cpad_r, bufC_r, bufG_r, gateA_r, _, _, _ = (
            sb(name + "_r", [P, KC, T + pad], F32R, mixer_mem) for name, pad in MIXER)
        vecs = bufB[0:NROW, 0:4, :].rearrange("p a b -> p (a b)")
        xn = bufD[:, :, :].rearrange("p (t a) b -> p t (a b)", t=TC)
        lruw = gateB[:, :, :].rearrange("p (w a) (h j) -> p w (a h) j", w=2, h=2)
        lsc = sb("lsc", [P, 8, KC], F32, mixer_mem)
        cacc = sb("cacc", [P, 2, T], F32, mixer_mem)
        lnw = sb("lnw", [P, 3, T], F32, mixer_mem)
        mixer_mem.close()
        moe_mem = stack
        xslot = sb("xslot", [P, KC, QUAD * SLOTS], F32, moe_mem)
        hn_hi = sb("hn_hi", [P, TC, D], F32R, moe_mem)
        hn_lo = sb("hn_lo", [P, TC, D], F32R, moe_mem)
        sel = sb("sel", [P, TC, QUAD * SLOTS], F32R, moe_mem)
        y_hi = sb("y_hi", [P, D], F32R, moe_mem)
        y_lo = sb("y_lo", [P, D], F32R, moe_mem)
        sgate = sb("sgate", [P, FE], F32, moe_mem)
        hid = sb("hid", [P, FE], F32, moe_mem)
        hidT = sb("hidT", [P, FC, P], F32, moe_mem)
        logit = sb("logit", [P, TC, NG + NE], F32, moe_mem)
        rt = sb("rt", [P, 12, TC, NE], F32, moe_mem)
        comb_hl = sb("comb_hl", [P, TC, NE, 2], F32R, moe_mem)
        rank = sb("rank", [P, TC, NE + QUAD], F32, moe_mem)
        rank_q = sb("rank_q", [QUAD, NQ, T], BF16, moe_mem)
        scrap = sb("scrap", [P, D], F32, moe_mem)
        rankT = sb("rankT", [NE, T], BF16, moe_mem)
        gfin = sb("gfin", [P, D], F32, moe_mem)
        ps = stack.enter_context(nc.psum_tensor("ps", [P, 8, 512], F32))

        x_in = [sem(f"x_in{tc}") for tc in range(TC)]
        vec_in = sem("vec_in")
        lruw_in = sem("lruw_in")
        router_in = sem("router_in")
        gfin_in = sem("gfin_in")
        mixw_full = [sem(f"mixw_full{i}") for i in range(SEG)]
        ex_full = [sem(f"ex_full{i}") for i in range(EXSLOTS)]
        out_done = sem("out_done")
        gp_step = sem("gp_step")
        dve_step = sem("dve_step")
        act_step = sem("act_step")
        dve_xn = sem("dve_xn")
        pe_par = sem("pe_par")
        par_ready = sem("par_ready")
        act_ssq = sem("act_ssq")
        dve_var = sem("dve_var")
        act_std = sem("act_std")
        act_whi = sem("act_whi")
        dve_wlo = sem("dve_wlo")
        act_split = sem("act_split")
        dve_split = sem("dve_split")
        act_lexp = sem("act_lexp")
        dve_labs = sem("dve_labs")
        dve_lsc = sem("dve_lsc")
        pe_chunk = sem("pe_chunk")
        act_evac = sem("act_evac")
        dve_conv4 = sem("dve_conv4")
        pe_lru = sem("pe_lru")
        act_lru = sem("act_lru")
        dve_lru = sem("dve_lru")
        dve_cmul = sem("dve_cmul")
        dve_conv = sem("dve_conv")
        pe_sum = sem("pe_sum")
        dve_cent = sem("dve_cent")
        act_sq = sem("act_sq")
        dve_norm = sem("dve_norm")
        act_silu = sem("act_silu")
        dve_yb = sem("dve_yb")
        pe_wout = sem("pe_wout")
        dve_h = sem("dve_h")
        pe_hT = sem("pe_hT")
        act_hT = sem("act_hT")
        dve_gw = sem("dve_gw")
        pe_logit = sem("pe_logit")
        dve_rstd2 = sem("dve_rstd2")
        act_hn = sem("act_hn")
        dve_hn = sem("dve_hn")
        dve_route = sem("dve_route")
        act_rexp = sem("act_rexp")
        pe_rank = sem("pe_rank")
        dve_mask = sem("dve_mask")
        dve_rank = sem("dve_rank")
        pe_rankT = sem("pe_rankT")
        dve_comb = sem("dve_comb")
        dve_rankT = sem("dve_rankT")
        rounds_ready = sem("rounds_ready")
        rankq_in = sem("rankq_in")
        pe_scat = sem("pe_scat")
        dve_sel = sem("dve_sel")
        pe_gather = sem("pe_gather")
        act_xslot = sem("act_xslot")
        pe_bc = sem("pe_bc")
        dve_selT = sem("dve_selT")
        pe_gu = sem("pe_gu")
        act_sg = sem("act_sg")
        dve_hid = sem("dve_hid")
        pe_ws = sem("pe_ws")
        dve_ws = sem("dve_ws")
        pe_hidT = sem("pe_hidT")
        act_hidT = sem("act_hidT")
        pe_down = sem("pe_down")
        act_yhi = sem("act_yhi")
        dve_ylo = sem("dve_ylo")
        dve_fin = sem("dve_fin")
        act_fssq = sem("act_fssq")
        act_fstd = sem("act_fstd")
        dve_out = sem("dve_out")

        x_v = x.rearrange("b (t p) d -> p (b t) d", p=P)
        out_v = out.rearrange("b (t p) d -> p (b t) d", p=P)

        def rows_by_chunk(w):
            return w.rearrange("(k p) n -> p k n", p=P)

        win_v = rows_by_chunk(w_in[0])
        tail_v = [rows_by_chunk(w[0]) for w in (w_rnn_out, w_conf_out, w_out)]
        SEG_RNN, SEG_GELU, SEG_CVAL, SEG_CGATE, SEG_GA, SEG_GB = range(6)

        def slot_kn(t, s):
            return t[:, s, :].rearrange("p (k n) -> p k n", k=KC)

        param_rows = [(R_GMIX, g_mix), (R_CCW, conf_conv_w[0]), (R_RCW, rnn_conv_w[0]), (R_RCB, rnn_conv_b),
                      (R_CCB, conf_conv_b), (R_GFFN, g_ffn),
                      (R_BR, lru_b_r.rearrange("l h j -> l (h j)")),
                      (R_BI, lru_b_i.rearrange("l h j -> l (h j)")), (R_A, lru_a_param),
                      (R_LNG, conf_ln_g), (R_LNB, conf_ln_b)]

        block = stack.enter_context(nc.Block())

        @block.sync
        def _(sp):
            for tc in range(TC):
                sp.dma_start(hres[:, tc, :], x_v[:, tc, :]).then_inc(x_in[tc], 16)
            for r, v in param_rows[:5]:
                sp.dma_start(vecs[r:r + v.shape[0], :], v).then_inc(vec_in, 16)

            def expert_panels(q, pair):
                for j in range(2):
                    e = q * QUAD + (2 * pair + j)
                    yield 6 * pair + 2 * j, w_gate, e
                    yield 6 * pair + 2 * j + 1, w_up, e
                for j in range(2):
                    yield 6 * pair + 4 + j, w_down, q * QUAD + (2 * pair + j)

            def load_expert(s, w, e):
                if w is w_down:
                    src = w[0, bass.ds(e, 1), :, :].rearrange("a (f p) n -> p (a f) n", p=P)
                    dst = ring[:, s, :].rearrange("p (f n) -> p f n", f=FC)
                else:
                    src = w[0, bass.ds(e, 1), :, :].rearrange("a (k p) n -> p (a k) n", p=P)
                    dst = slot_kn(ring, s)
                sp.dma_start(dst, src).then_inc(ex_full[s], 16)

            first = [p for pair in range(2) for p in expert_panels(0, pair)]
            order = [(seg, p) for p in range(SEG) for seg in (SEG_CVAL, SEG_CGATE)]
            order += [(seg, p) for seg in (SEG_RNN, SEG_GELU, SEG_GA, SEG_GB, 6, 7, 8) for p in range(SEG)]
            for k in range(NMIX):
                if k >= SEG:
                    sp.wait_ge(pe_chunk, KC + 2 * (k - SEG + 1))
                seg, p = order[k]
                if seg < 6:
                    src = win_v[:, :, seg * D + p * PN: seg * D + (p + 1) * PN]
                else:
                    src = tail_v[seg - 6][:, :, p * PN:(p + 1) * PN]
                sp.dma_start(slot_kn(ring, MIX_SLOT + k % SEG), src).then_inc(mixw_full[k % SEG], 16)
                if k >= K_RNN and k % 2 == 0 and first[0][0] < HI_SLOT:
                    load_expert(*first.pop(0))
            for s, w, e in sorted(first, key=lambda panel: panel[0]):
                if s < MIX_SLOT:
                    sp.wait_ge(pe_wout, 2 * (s - HI_SLOT + 1))
                load_expert(s, w, e)
            sp.wait_ge(dve_rankT, 1)
            for q in range(NQ):
                sp.dma_start(rank_q[:, q, :], rankT[q * QUAD:(q + 1) * QUAD, :]).then_inc(rankq_in, 16)
            sp.wait_ge(rounds_ready, 1)
            n_rounds = nc.values_load(rounds[0:1, 0:1], engines=[ENG.SP], min_val=1, max_val=4)
            with loop(ENG.SP, 1, n_rounds * NQ) as g:
                q = g % NQ
                for pair in range(2):
                    for k, (s, w, e) in enumerate(expert_panels(q, pair)):
                        if k == 0:
                            sp.wait_ge(pe_gu, (g - 1) * 2 + (pair + 1))
                        if k == 4:
                            sp.wait_ge(pe_down, (g - 1) * 2 + (pair + 2))
                        load_expert(s, w, e)
            for tc in range(TC):
                sp.wait_ge(dve_out, tc + 1)
                sp.dma_start(out_v[:, tc, :], hres[:, tc, :]).then_inc(out_done, 16)
            sp.wait_ge(out_done, 16 * TC)

        @block.gpsimd
        def _(gp):
            gp.dma_start(lruw[:, 0, :, :], lru_w_r[0].rearrange("h i j -> i h j")).then_inc(lruw_in, 16)
            gp.dma_start(lruw[:, 1, :, :], lru_w_i[0].rearrange("h i j -> i h j")).then_inc(lruw_in, 16)
            gp.dma_start(wrt[:, :, 0:NG], rows_by_chunk(w_group_router[0])).then_inc(router_in, 16)
            gp.dma_start(wrt[:, :, NG:], rows_by_chunk(w_expert_router[0])).then_inc(router_in, 16)
            gp.dma_start(brt[:, 0:NG], bcast(b_group_router, 0, P)).then_inc(router_in, 16)
            gp.dma_start(brt[:, NG:], bcast(b_expert_router, 0, P)).then_inc(router_in, 16)
            n = [0]

            def link(ins):
                n[0] += 1
                ins.then_inc(gp_step, 1)
                gp.wait_ge(gp_step, n[0])

            link(gp.memset(ident[:, :], 0.0))
            link(gp.memset(ones[:, :], 1.0))
            link(gp.affine_select(out=ident[:, :], in_=ident[:, :], compare_op=ALU.not_equal, fill=1.0, base=0,
                                  pattern=[[-1, P]], channel_multiplier=1))
            link(gp.affine_select(out=tri[:, :], in_=ones[:, :], compare_op=ALU.is_gt, fill=0.0, base=0,
                                  pattern=[[1, P]], channel_multiplier=-1))
            link(gp.memset(bufA[:, :, 0:RNNW - 1], 0.0))
            link(gp.memset(cpad[:, :, 0:CONVW - 1], 0.0))
            link(gp.iota(iota_s[:, :], pattern=[[1, SLOTS]], base=1, channel_multiplier=0,
                         allow_small_or_imprecise_dtypes=True))
            link(gp.iota(desc[:, :], pattern=[[-1, NE]], base=NE, channel_multiplier=0,
                         allow_small_or_imprecise_dtypes=True))
            for half in (slice(0, SLOTS), slice(SLOTS, P)):
                link(gp.iota(slot_no[half, :], pattern=[[0, 1]], base=1, channel_multiplier=1,
                             allow_small_or_imprecise_dtypes=True))
            link(gp.tensor_scalar(selT[:, :, :].rearrange("p a (b t) -> p (a b) t", b=TC),
                                  bcast(ones[:, :].rearrange("p (a t) -> p a t", a=1), 1, 2 * TC),
                                  0.0, None, ALU.mult))
            gp.memset(wslot[:, :], 0.0).then_inc(dve_ws, 1)
            gp.wait_ge(dve_ws, 1)
            link(gp.memset(pair_row[:, :, :], 0.0))
            link(gp.affine_select(out=pair_row[:, :, :].rearrange("q a (b s) -> q (a b) s", b=2),
                                  in_=pair_row[:, :, :].rearrange("q a (b s) -> q (a b) s", b=2),
                                  compare_op=ALU.not_equal, fill=1.0, base=0,
                                  pattern=[[-1, QUAD], [0, SLOTS]], channel_multiplier=1))

        @block.scalar
        def _(act):
            for r, v in param_rows[5:]:
                act.dma_start(vecs[r:r + v.shape[0], :], v).then_inc(vec_in, 16)

            for tc in range(TC):
                act.wait_ge(x_in[tc], 16)
                act.activation(gateA[:, 4 * tc:4 * tc + 4, :].rearrange("p a b -> p (a b)"), hres[:, tc, :], ACT.Square,
                               accum_out=stat[:, tc:tc + 1]).then_inc(act_ssq, 1)
            act.wait_ge(dve_var, 1)
            act.activation(stat[:, 4:6], stat[:, 2:4], ACT.Sqrt).then_inc(act_std, 1)
            act.wait_ge(dve_labs, 1)
            act.activation(lsc[:, 1, :], lsc[:, 0, :], ACT.Exp, scale=-1.0).then_inc(act_lexp, 1)
            for c in range(KC):
                act.wait_ge(pe_chunk, c + 1)
                act.activation(actT[:, c, :], ps[:, c % 4, 0:T], ACT.Identity,
                               scale=par[:, c, R_GMIX:R_GMIX + 1]).then_inc(act_evac, 1)

            def take_segment(seg, func, dst, before=None):
                base = KC + KC * seg
                with loop(ENG.Activation, 0, KC // 4) as i:
                    for b in range(4):
                        if before:
                            before(i * 4 + b)
                        act.wait_ge(pe_chunk, i * 4 + (base + b + 1))
                        act.activation(dst(i * 4 + b), ps[:, b, 0:T], func).then_inc(act_evac, 1)

            def take_conformer(lo, hi):
                with loop(ENG.Activation, lo, hi) as i:
                    for b in range(4):
                        act.wait_ge(pe_chunk, i * 4 + (KC + b + 1))
                        c = bass.ds(i * 2 + b % 2, 1)
                        d = cpad[:, c, CONVW - 1:] if b < 2 else gateA[:, c, :]
                        act.activation(d.rearrange("p a b -> p (a b)"), ps[:, b, 0:T],
                                       ACT.Identity if b < 2 else ACT.Sigmoid).then_inc(act_evac, 1)

            def weight_hi(n):
                act.wait_ge(mixw_full[n % SEG], 16 * ((K_SPLIT + n) // SEG + 1))
                if n >= SEG:
                    act.wait_ge(pe_chunk, KC + 2 * (K_SPLIT + n - SEG + 1))
                act.activation(ring_r[:, HI_SLOT + n % SEG, :], ring[:, MIX_SLOT + n % SEG, :], ACT.Copy
                               ).then_inc(act_whi, 1)

            def take_panel(k, func, dst, before=None):
                for m in (2 * k, 2 * k + 1):
                    c = m % KC
                    act.wait_ge(pe_chunk, KC + m + 1)
                    if before:
                        before(c)
                    act.activation(dst[:, c, 0:T], ps[:, m % 4, 0:T], func).then_inc(act_evac, 1)

            def take_ga(p):
                take_panel(K_SPLIT + p, ACT.Sigmoid, gateA, before=lambda c: act.wait_ge(dve_cmul, c + 1))

            def take_gb(p):
                take_panel(K_SPLIT + SEG + p, ACT.Sigmoid, gateB)

            def take_ya(p):
                take_panel(K_SPLIT + 2 * SEG + p, ACT.Identity, bufD)

            take_conformer(0, SEG)
            take_segment(2, ACT.Identity,
                         lambda c: bufA[:, bass.ds(c, 1), RNNW - 1:].rearrange("p a b -> p (a b)"))
            act.wait_ge(act_evac, KC)
            act.activation(u_hi[:, :, :], actT[:, :, :], ACT.Copy).then_inc(act_split, 1)
            for p in range(SEG):
                if p >= 2:
                    weight_hi(p - 2)
                take_panel(K_GELU + p, ACT.Gelu_apprx_tanh, bufG)
            for m in range(2 * KC):
                c, w = m // 2, m % 2
                act.wait_ge(pe_lru, m + 1)
                row = (R_BR, R_BI)[w]
                act.activation((bufC, bufD)[w][:, c, :], ps[:, 4 + m % 4, 0:T], ACT.Sigmoid,
                               bias=par[:, c, row:row + 1]).then_inc(act_lru, 1)
            weight_hi(2)
            take_ga(0)
            act.wait_ge(dve_lsc, 1)
            act.wait_ge(act_lru, 2 * KC)
            act.wait_ge(dve_conv4, KC)
            for c in range(KC):
                act.activation(bufA[:, c, 0:T], bufC[:, c, :], ACT.Tanh, scale=lsc[:, 7, c:c + 1]
                               ).then_inc(act_lru, 1)
            for c in range(KC):
                act.wait_ge(act_lru, 2 * KC + c + 1)
                act.activation(bufC[:, c, :], bufC[:, c, :], ACT.Exp, scale=lsc[:, 7, c:c + 1]
                               ).then_inc(act_lru, 1)
            weight_hi(3)
            take_ga(1)
            weight_hi(4)
            act.wait_ge(dve_lru, 1)
            act.wait_ge(act_lru, 4 * KC)
            act.activation(bufB[:, :, :], bufC[:, :, :], ACT.Square).then_inc(act_lru, 1)
            take_ga(2)
            weight_hi(5)
            act.wait_ge(dve_lru, 2)
            act.activation(bufA[:, :, 0:T], bufB[:, :, :], ACT.Sqrt, scale=-1.0).then_inc(act_lru, 1)
            take_ga(3)
            weight_hi(6)
            take_gb(0)
            act.wait_ge(dve_lru, 4)
            act.activation(bufA_r[:, :, 0:T], bufG[:, :, :], ACT.Copy).then_inc(act_split, 1)
            act.wait_ge(dve_cent, 1)
            act.activation(bufB[:, :, :], cpad[:, :, CONVW - 1:], ACT.Square).then_inc(act_sq, 1)
            weight_hi(7)
            take_gb(1)
            weight_hi(8)
            take_gb(2)
            act.wait_ge(dve_cent, 2)
            act.activation(lnw[:, 2, :], lnw[:, 1, :], ACT.Sqrt).then_inc(act_sq, 1)
            weight_hi(9)
            take_gb(3)
            weight_hi(10)
            take_ya(0)
            act.wait_ge(dve_norm, 1)
            for c in range(KC):
                act.activation(bufC[:, c, :], cpad[:, c, CONVW - 1:], ACT.Silu, scale=par[:, c, R_LNG:R_LNG + 1],
                               bias=par[:, c, R_LNB:R_LNB + 1]).then_inc(act_silu, 1)
            weight_hi(11)
            take_ya(1)
            act.wait_ge(act_silu, KC)
            act.activation(cpad_r[:, :, 0:T], bufC[:, :, :], ACT.Copy).then_inc(act_split, 1)
            weight_hi(12)
            take_ya(2)
            weight_hi(13)
            take_ya(3)
            for p in range(SEG):
                weight_hi(3 * SEG + 2 + p)
                for c in (2 * p, 2 * p + 1):
                    act.wait_ge(dve_yb, 2 * c + 2)
                    act.activation(bufA_r[:, c, 0:T], gateA[:, c, :], ACT.Copy).then_inc(act_split, 1)
            weight_hi(4 * SEG + 2)
            weight_hi(4 * SEG + 3)

            def squares(p):
                for tc in range(TC):
                    act.wait_ge(dve_h, 2 * p + tc + 1)
                    act.activation(bufC[:, 2 * p + tc, :], hres[:, tc, p * PN:(p + 1) * PN], ACT.Square,
                                   accum_out=ssp[:, tc, p:p + 1]).then_inc(act_ssq, 1)

            def take_hT(p):
                for c in (2 * p, 2 * p + 1):
                    act.wait_ge(pe_hT, c + 1)
                    act.activation(actT[:, c, :], ps[:, c % 2, 0:T], ACT.Identity).then_inc(act_hT, 1)

            for p in range(SEG):
                squares(p)
                if p:
                    take_hT(p - 1)
            act.wait_ge(dve_var, 2)
            act.activation(stat[:, 4:6], stat[:, 2:4], ACT.Sqrt).then_inc(act_std, 1)
            take_hT(SEG - 1)
            act.wait_ge(dve_rstd2, 1)
            for tc in range(TC):
                act.activation(hn_hi[:, tc, :], hres[:, tc, :], ACT.Copy, scale=stat[:, 6 + tc:7 + tc]
                               ).then_inc(act_hn, 1)
            act.wait_ge(dve_route, 1)
            act.activation(rt[:, 1, :, 0:NG], rt[:, 0, :, 0:NG], ACT.Exp).then_inc(act_rexp, 1)
            act.wait_ge(dve_route, 2)
            act.activation(stat[:, 2:4], stat[:, 8:10], ACT.Exp).then_inc(act_rexp, 1)
            act.dma_start(gfin[:, :], bcast(g_final.rearrange("(a d) -> a d", a=1), 0, P)).then_inc(gfin_in, 16)

            act.wait_ge(rounds_ready, 1)
            n_rounds = nc.values_load(rounds[0:1, 0:1], engines=[ENG.Activation],
                                      min_val=1, max_val=4)

            def weighted_hi(pair, downs, weights):
                act.wait_ge(pe_down, downs)
                act.wait_ge(dve_ws, weights)
                act.activation(y_hi[:, :], ps[:, 6:8, :].rearrange("p a b -> p (a b)"), ACT.Copy,
                               scale=wslot[:, pair:pair + 1]).then_inc(act_yhi, 1)

            with loop(ENG.Activation, 0, n_rounds * NQ) as g:
                for c in range(KC):
                    act.wait_ge(pe_gather, g * KC + (c + 1))
                    act.activation(xslot[:, c, :], ps[:, 4 + c % 2, 0:T], ACT.Copy,
                                   scale=par[:, c, R_GFFN:R_GFFN + 1]).then_inc(act_xslot, 1)
                weighted_hi(1, g * 2 + 1, g * 4 + 1)
                for pair in range(2):
                    act.wait_ge(pe_gu, g * 2 + (pair + 1))
                    act.activation(sgate[:, :], ps[:, 4, 0:FE], ACT.Silu).then_inc(act_sg, 1)
                    act.wait_ge(pe_hidT, g * 2 + (pair + 1))
                    act.activation(hidT[:, :, :].rearrange("p a b -> p (a b)"), ps[:, 4, 0:FE], ACT.Copy
                                   ).then_inc(act_hidT, 1)
                    if pair == 0:
                        weighted_hi(0, g * 2 + 2, g * 4 + 3)
            weighted_hi(1, n_rounds * (2 * NQ) + 1, n_rounds * (4 * NQ) + 1)
            for tc in range(TC):
                act.wait_ge(dve_fin, tc + 1)
                if tc:
                    act.wait_ge(act_fssq, tc)
                act.activation(scrap[:, :], hres[:, tc, :], ACT.Square, accum_out=stat[:, tc:tc + 1]
                               ).then_inc(act_fssq, 1)
            act.wait_ge(dve_fin, TC + 1)
            act.activation(stat[:, 4:6], stat[:, 2:4], ACT.Sqrt).then_inc(act_fstd, 1)

        @block.vector
        def _(v):
            n = [0]

            def step(ins):
                n[0] += 1
                ins.then_inc(dve_step, 1)
                return n[0]

            def link(ins):
                v.wait_ge(dve_step, step(ins))

            v.wait_ge(act_ssq, TC)
            v.tensor_scalar(stat[:, 2:4], stat[:, 0:2], 1.0 / D, RMS_EPS, ALU.mult, ALU.add
                            ).then_inc(dve_var, 1)
            v.wait_ge(act_std, 1)
            link(v.reciprocal(stat[:, 6:8], stat[:, 4:6]))
            for tc in range(TC):
                v.tensor_scalar(xn[:, tc, :], hres[:, tc, :], stat[:, 6 + tc:7 + tc], None, ALU.mult
                                ).then_inc(dve_xn, 1)
            v.wait_ge(pe_par, 1)
            v.tensor_copy(par[:, :, :].rearrange("p k r -> p (k r)"), ps[:, 7, 0:KC * NROW]).then_inc(par_ready, 1)
            v.wait_ge(par_ready, 1)
            a_par = par[:, :, R_A:R_A + 1].rearrange("p k r -> p (k r)")
            link(v.tensor_scalar(lsc[:, 2, :], a_par, -1.0, None, ALU.mult))
            v.tensor_tensor(lsc[:, 0, :], lsc[:, 2, :], a_par, ALU.max).then_inc(dve_labs, 1)
            v.wait_ge(act_lexp, 1)
            link(v.tensor_scalar(lsc[:, 2, :], lsc[:, 1, :], 2.0, None, ALU.add))
            link(v.reciprocal(lsc[:, 3, :], lsc[:, 2, :]))
            link(v.tensor_tensor(lsc[:, 4, :], lsc[:, 1, :], lsc[:, 3, :], ALU.mult))
            link(v.tensor_tensor(lsc[:, 5, :], lsc[:, 4, :], lsc[:, 4, :], ALU.mult))
            link(v.tensor_scalar(lsc[:, 6, :], lsc[:, 5, :], 1.0 / 19, None, ALU.mult))
            for odd in (17, 15, 13, 11, 9, 7, 5, 3):
                link(v.scalar_tensor_tensor(out=lsc[:, 6, :], in0=lsc[:, 6, :], scalar=1.0 / odd,
                                            in1=lsc[:, 5, :], op0=ALU.add, op1=ALU.mult))
            link(v.scalar_tensor_tensor(out=lsc[:, 6, :], in0=lsc[:, 6, :], scalar=1.0,
                                        in1=lsc[:, 4, :], op0=ALU.add, op1=ALU.mult))
            link(v.tensor_scalar(lsc[:, 3, :], a_par, 0.0, LRU_C, ALU.min, ALU.mult))
            v.scalar_tensor_tensor(out=lsc[:, 7, :], in0=lsc[:, 6, :], scalar=-2.0 * LRU_C,
                                   in1=lsc[:, 3, :], op0=ALU.mult, op1=ALU.add).then_inc(dve_lsc, 1)
            v.wait_ge(router_in, 64)
            for c in range(KC):
                v.tensor_scalar(wrt[:, c, :], wrt[:, c, :], par[:, c, R_GFFN:R_GFFN + 1], None, ALU.mult
                                ).then_inc(dve_gw, 1)

            def conv(lo, hi, src, acc, dst, taps, w_row, b_row, before, done, halfway=None):
                per = 2 * (taps - 1)
                base = n[0] - lo * per
                with loop(ENG.DVE, lo, hi) as i:
                    before(i)
                    for k in range(taps):
                        if halfway and k == taps // 2:
                            halfway()
                        for j in range(2):
                            c = bass.ds(i * 2 + j, 1)
                            s = src[:, c, k:k + T].rearrange("p a b -> p (a b)")
                            a, d = (x(c, j).rearrange("p a b -> p (a b)") for x in (acc, dst))
                            w = par[:, c, w_row + k:w_row + k + 1].rearrange("p a b -> p (a b)")
                            if k == 0:
                                b = par[:, c, b_row:b_row + 1].rearrange("p a b -> p (a b)")
                                ins = v.tensor_scalar(a, s, w, b, ALU.mult, ALU.add)
                            else:
                                v.wait_ge(dve_step, i * per + (base + 2 * (k - 1) + j + 1))
                                ins = v.scalar_tensor_tensor(out=d if k == taps - 1 else a, in0=s, scalar=w,
                                                             in1=a, op0=ALU.mult, op1=ALU.add)
                            ins.then_inc(done if k == taps - 1 else dve_step, 1)
                n[0] += per * (hi - lo)

            def gated(i):
                v.wait_ge(act_evac, i * 4 + (KC + 4))
                for j in range(2):
                    cc = bass.ds(i * 2 + j, 1)
                    c = cpad[:, cc, CONVW - 1:].rearrange("p a b -> p (a b)")
                    v.tensor_tensor(c, c, gateA[:, cc, :].rearrange("p a b -> p (a b)"), ALU.mult
                                    ).then_inc(dve_cmul, 1)
                v.wait_ge(dve_cmul, i * 2 + 2)

            def conformer_conv(lo, hi, halfway=None):
                conv(lo, hi, cpad, lambda c, j: cacc[:, j:j + 1, :], lambda c, j: cpad[:, c, CONVW - 1:],
                     CONVW, R_CCW, R_CCB, gated, dve_conv, halfway)

            def weight_lo(n):
                v.wait_ge(act_whi, n + 1)
                v.tensor_tensor(ring_r[:, MIX_SLOT + n % SEG, :], ring[:, MIX_SLOT + n % SEG, :],
                                ring_r[:, HI_SLOT + n % SEG, :].bitcast(F32), ALU.subtract).then_inc(dve_wlo, 1)

            def operand_lo(count, lo, full, hi):
                v.wait_ge(act_split, count)
                v.tensor_tensor(lo, full, hi.bitcast(F32), ALU.subtract).then_inc(dve_split, 1)

            v.wait_ge(gp_step, 13)
            conformer_conv(0, 3)
            conv(0, KC // 2, bufA, lambda c, j: bufB[:, c, :], lambda c, j: bufB[:, c, :], RNNW, R_RCW, R_RCB,
                 lambda i: v.wait_ge(act_evac, i * 2 + (3 * KC + 2)), dve_conv4)
            operand_lo(1, u_lo[:, :, :], actT[:, :, :], u_hi[:, :, :])
            weight_lo(0)
            weight_lo(1)
            conformer_conv(3, 4, halfway=lambda: weight_lo(2))
            weight_lo(3)
            v.wait_ge(act_lru, 2 * KC)
            v.wait_ge(dve_conv4, KC)
            v.tensor_tensor(bufD[:, :, :], bufD[:, :, :], bufB[:, :, :], ALU.mult).then_inc(dve_lru, 1)
            weight_lo(4)
            v.wait_ge(act_lru, 4 * KC + 1)
            v.scalar_tensor_tensor(out=bufB[:, :, :], in0=bufB[:, :, :], scalar=1.0, in1=bufA[:, :, 0:T],
                                   op0=ALU.add, op1=ALU.mult).then_inc(dve_lru, 1)
            weight_lo(5)
            v.wait_ge(act_lru, 4 * KC + 2)
            v.tensor_tensor(bufD[:, :, :], bufD[:, :, :], bufA[:, :, 0:T], ALU.mult).then_inc(dve_lru, 1)
            v.wait_ge(dve_lru, 3)
            for c in range(KC):
                last = step(v.tensor_tensor_scan(bufB[:, c, :], bufC[:, c, :], bufD[:, c, :], 0.0,
                                                 ALU.mult, ALU.add))
            v.wait_ge(dve_step, last)
            v.wait_ge(act_evac, 5 * KC)
            v.tensor_tensor(bufG[:, :, :], bufG[:, :, :], bufB[:, :, :], ALU.mult).then_inc(dve_lru, 1)
            centred = cpad[:, :, CONVW - 1:]
            v.wait_ge(pe_sum, 1)
            link(v.tensor_scalar(lnw[:, 0, :], ps[:, 4, 0:T], 1.0 / D, None, ALU.mult))
            v.tensor_tensor(centred, centred, bcast(lnw[:, 0:1, :], 1, KC), ALU.subtract).then_inc(dve_cent, 1)
            weight_lo(6)
            operand_lo(2, bufG_r[:, :, :], bufG[:, :, :], bufA_r[:, :, 0:T])
            weight_lo(7)
            weight_lo(8)
            v.wait_ge(pe_sum, 2)
            v.tensor_scalar(lnw[:, 1, :], ps[:, 5, 0:T], 1.0 / D, LN_EPS, ALU.mult, ALU.add).then_inc(dve_cent, 1)
            weight_lo(9)
            v.wait_ge(act_sq, 2)
            link(v.reciprocal(lnw[:, 0, :], lnw[:, 2, :]))
            v.tensor_tensor(centred, centred, bcast(lnw[:, 0:1, :], 1, KC), ALU.mult).then_inc(dve_norm, 1)
            weight_lo(10)
            weight_lo(11)
            operand_lo(3, bufC_r[:, :, :], bufC[:, :, :], cpad_r[:, :, 0:T])
            weight_lo(12)
            weight_lo(13)
            v.wait_ge(act_evac, 8 * KC)
            link(v.tensor_tensor(gateA[:, :, :], gateA[:, :, :], bufD[:, :, :], ALU.mult))
            for p in range(SEG):
                weight_lo(3 * SEG + 2 + p)
                for c in (2 * p, 2 * p + 1):
                    v.wait_ge(pe_chunk, KC + 7 * KC + c + 1)
                    v.tensor_tensor(gateB[:, c, :], gateB[:, c, :], ps[:, c % 4, 0:T], ALU.mult).then_inc(dve_yb, 1)
                    v.wait_ge(dve_yb, 2 * c + 1)
                    v.tensor_tensor(gateA[:, c, :], gateA[:, c, :], gateB[:, c, :], ALU.add).then_inc(dve_yb, 1)
                for c in (2 * p, 2 * p + 1):
                    operand_lo(4 + c, gateA_r[:, c, :], gateA[:, c, :], bufA_r[:, c, 0:T])
            weight_lo(4 * SEG + 2)
            weight_lo(4 * SEG + 3)
            for p in range(SEG):
                for tc in range(TC):
                    v.wait_ge(pe_wout, 2 * p + tc + 1)
                    hcol = hres[:, tc, p * PN:(p + 1) * PN]
                    v.tensor_tensor(hcol, hcol, ps[:, 4 + tc, 0:PN], ALU.add).then_inc(dve_h, 1)
            v.wait_ge(act_ssq, TC + 2 * SEG)
            link(v.tensor_reduce(stat[:, 0:2], ssp[:, :, :], AX, ALU.add))
            v.tensor_scalar(stat[:, 2:4], stat[:, 0:2], 1.0 / D, RMS_EPS, ALU.mult, ALU.add).then_inc(dve_var, 1)
            v.wait_ge(act_std, 2)
            v.reciprocal(stat[:, 6:8], stat[:, 4:6]).then_inc(dve_rstd2, 1)
            v.wait_ge(dve_rstd2, 1)

            def col(k):
                return stat[:, k:k + TC].rearrange("p (t a) -> p t a", a=1)

            v.wait_ge(pe_logit, 1)
            for tc in range(TC):
                last = step(v.scalar_tensor_tensor(out=logit[:, tc, :], in0=ps[:, 2 + tc, 0:NG + NE],
                                                   scalar=stat[:, 6 + tc:7 + tc], in1=brt[:, :],
                                                   op0=ALU.mult, op1=ALU.add))
            v.wait_ge(dve_step, last)
            gl = logit[:, :, 0:NG]
            el = logit[:, :, NG:NG + NE]

            def first_of(dst, src, top, width, tmp):
                link(v.tensor_tensor(rt[:, tmp, :, 0:width], src, bcast(top, 2, width), ALU.is_equal))
                d = bcast(desc[:, 0:width].rearrange("p (a w) -> p a w", a=1), 1, TC)
                link(v.tensor_tensor(rt[:, tmp, :, 0:width], rt[:, tmp, :, 0:width], d, ALU.mult))
                link(v.tensor_reduce(stat[:, 14:16], rt[:, tmp, :, 0:width], AX, ALU.max))
                link(v.tensor_tensor(dst, rt[:, tmp, :, 0:width], bcast(col(14), 2, width), ALU.is_equal))

            link(v.tensor_reduce(stat[:, 12:14], gl, AX, ALU.max))
            v.tensor_tensor(rt[:, 0, :, 0:NG], gl, bcast(col(12), 2, NG), ALU.subtract).then_inc(dve_route, 1)
            first_of(rt[:, 2, :, 0:NG], gl, col(12), NG, 3)
            link(v.tensor_scalar(rt[:, 3, :, 0:NG], rt[:, 2, :, 0:NG], -1.0, 1e30, ALU.add, ALU.mult))
            e4 = rt[:, 4, :, :].rearrange("p t (g e) -> p (t g) e", g=NG)
            for tc in range(TC):
                drop = bcast(rt[:, 3, tc, 0:NG].rearrange("p (g a) -> p g a", a=1), 2, PER_GROUP)
                last = step(v.tensor_tensor(rt[:, 4, tc, :].rearrange("p (g e) -> p g e", g=NG),
                                            logit[:, tc, NG:].rearrange("p (g e) -> p g e", g=NG),
                                            drop, ALU.add))
            v.wait_ge(dve_step, last)
            link(v.tensor_reduce(stat[:, 12:14], rt[:, 4, :, :], AX, ALU.max))
            first_of(rt[:, 5, :, :], rt[:, 4, :, :], col(12), NE, 6)
            link(v.scalar_tensor_tensor(out=rt[:, 7, :, :], in0=rt[:, 5, :, :], scalar=-2e30,
                                        in1=rt[:, 4, :, :], op0=ALU.mult, op1=ALU.add))
            link(v.tensor_reduce(stat[:, 10:12], rt[:, 7, :, :], AX, ALU.max))
            v.tensor_tensor(stat[:, 8:10], stat[:, 10:12], stat[:, 12:14], ALU.subtract).then_inc(dve_route, 1)
            first_of(rt[:, 8, :, :], rt[:, 7, :, :], col(10), NE, 6)
            v.tensor_tensor(rt[:, 9, :, :], rt[:, 5, :, :], rt[:, 8, :, :], ALU.add).then_inc(dve_mask, 1)
            for tc in range(TC):
                v.wait_ge(act_hn, tc + 1)
                v.scalar_tensor_tensor(out=hn_lo[:, tc, :], in0=hres[:, tc, :], scalar=stat[:, 6 + tc:7 + tc],
                                       in1=hn_hi[:, tc, :].bitcast(F32), op0=ALU.mult, op1=ALU.subtract
                                       ).then_inc(dve_hn, 1)
            v.wait_ge(pe_rank, 1)
            for tc in range(TC):
                last = step(v.scalar_tensor_tensor(out=rank[:, tc, 0:NE], in0=ps[:, 6, NE * tc:NE * (tc + 1)],
                                                   scalar=1.0, in1=rt[:, 9, tc, :], op0=ALU.add, op1=ALU.mult))
            v.wait_ge(dve_step, last)
            v.tensor_scalar(rank[:, :, NE:], rank[:, :, 0:QUAD], -float(SLOTS), None, ALU.add
                            ).then_inc(dve_rank, 1)
            link(v.tensor_reduce(stat[:, 12:13], ps[:, 6, 2 * NE:3 * NE], AX, ALU.max))
            link(v.tensor_scalar(stat[:, 13:14], stat[:, 12:13], float(SLOTS), 1.0, ALU.is_gt, ALU.add))
            for k in range(2, T // SLOTS):
                link(v.scalar_tensor_tensor(out=stat[:, 13:14], in0=stat[:, 12:13], scalar=float(k * SLOTS),
                                            in1=stat[:, 13:14], op0=ALU.is_gt, op1=ALU.add))
            v.tensor_copy(rounds[:, :], stat[:, 13:14]).then_inc(rounds_ready, 1)

            def fill_sel(q):
                for tc in range(TC):
                    ins = v.tensor_tensor(
                        sel[:, tc, :].rearrange("p (e s) -> p e s", s=SLOTS),
                        bcast(rank[:, tc, q].rearrange("p (e a) -> p e a", a=1), 2, SLOTS),
                        bcast(iota_s[:, :].rearrange("p (a s) -> p a s", a=1), 1, QUAD), ALU.is_equal)
                return ins

            v.wait_ge(dve_rank, 1)
            fill_sel(slice(0, QUAD)).then_inc(dve_sel, 1)
            v.wait_ge(pe_rankT, 1)
            v.tensor_copy(rankT[:, :], ps[0:NE, 7, 0:T]).then_inc(dve_rankT, 1)
            v.wait_ge(act_rexp, 1)
            v.wait_ge(rounds_ready, 1)
            link(v.tensor_reduce(stat[:, 12:14], rt[:, 1, :, 0:NG], AX, ALU.add))
            v.wait_ge(act_rexp, 2)
            link(v.scalar_tensor_tensor(out=stat[:, 14:16], in0=stat[:, 2:4], scalar=1.0,
                                        in1=stat[:, 12:14], op0=ALU.add, op1=ALU.mult))
            link(v.reciprocal(stat[:, 12:14], stat[:, 14:16]))
            link(v.tensor_tensor(stat[:, 14:16], stat[:, 12:14], stat[:, 2:4], ALU.mult))
            link(v.tensor_tensor(rt[:, 5, :, :], rt[:, 5, :, :], bcast(col(12), 2, NE), ALU.mult))
            link(v.tensor_tensor(rt[:, 8, :, :], rt[:, 8, :, :], bcast(col(14), 2, NE), ALU.mult))
            link(v.tensor_tensor(rt[:, 10, :, :], rt[:, 5, :, :], rt[:, 8, :, :], ALU.add))
            hi = comb_hl[:, :, :, 0:1].rearrange("p t e a -> p t (e a)")
            lo = comb_hl[:, :, :, 1:2].rearrange("p t e a -> p t (e a)")
            link(v.tensor_copy(hi, rt[:, 10, :, :]))
            v.tensor_tensor(lo, rt[:, 10, :, :], hi.bitcast(F32), ALU.subtract).then_inc(dve_comb, 1)

            v.wait_ge(rounds_ready, 1)
            n_rounds = nc.values_load(rounds[0:1, 0:1], engines=[ENG.DVE], min_val=1, max_val=4)
            own = n[0]
            v.wait_ge(dve_ws, 1)

            def weighted_lo(pair, yhis):
                v.wait_ge(act_yhi, yhis)
                v.scalar_tensor_tensor(out=y_lo[:, :], in0=ps[:, 6:8, :].rearrange("p a b -> p (a b)"),
                                       scalar=wslot[:, pair:pair + 1], in1=y_hi[:, :].bitcast(F32),
                                       op0=ALU.mult, op1=ALU.subtract).then_inc(dve_ylo, 1)

            with loop(ENG.DVE, 0, n_rounds) as r:
                with loop(ENG.DVE, 0, NQ) as q:
                    g = r * NQ + q
                    weighted_lo(1, g * 2 + 1)
                    for pair in range(2):
                        v.wait_ge(pe_ws, g * 2 + (pair + 1))
                        for j in range(2):
                            half = slice(SLOTS * j, SLOTS * (j + 1))
                            v.tensor_reduce(wslot[half, pair:pair + 1], ps[half, 6, 2 * j:2 * j + 2], AX, ALU.add
                                            ).then_inc(dve_ws, 1)
                        v.wait_ge(act_sg, g * 2 + (pair + 1))
                        v.tensor_tensor(hid[:, :], sgate[:, :], ps[:, 4, FE:2 * FE], ALU.mult).then_inc(dve_hid, 1)
                        if pair == 0:
                            v.wait_ge(pe_bc, g + 1)
                            v.tensor_scalar(selT[:, :, :].rearrange("p a t -> p (a t)"), ps[:, 5, :],
                                            slot_no[:, 0:1], None, ALU.is_equal).then_inc(dve_selT, 1)
                            v.wait_ge(dve_ws, g * 4 + 3)
                            weighted_lo(0, g * 2 + 2)
                        else:
                            fill_sel(bass.ds((q + 1) * QUAD, QUAD)).then_inc(dve_sel, 1)
                v.wait_ge(dve_sel, (r + 1) * NQ + 1)
                v.tensor_scalar(rank[:, :, :], rank[:, :, :], -float(SLOTS), None, ALU.add).then_inc(dve_step, 1)
                v.wait_ge(dve_selT, (r + 1) * NQ)
                v.tensor_scalar(slot_no[:, :], slot_no[:, :], float(SLOTS), None, ALU.add).then_inc(dve_step, 1)
                v.wait_ge(dve_step, r * 2 + (own + 2))
            v.wait_ge(dve_ws, n_rounds * (4 * NQ) + 1)
            weighted_lo(1, n_rounds * (2 * NQ) + 1)
            v.wait_ge(pe_scat, n_rounds * (2 * NQ) + 1)
            for tc in range(TC):
                v.tensor_tensor(hres[:, tc, :], hres[:, tc, :],
                                ps[:, 2 * tc:2 * tc + 2, :].rearrange("p a b -> p (a b)"), ALU.add
                                ).then_inc(dve_fin, 1)
            v.wait_ge(act_fssq, TC)
            v.tensor_scalar(stat[:, 2:4], stat[:, 0:2], 1.0 / D, RMS_EPS, ALU.mult, ALU.add).then_inc(dve_fin, 1)
            v.wait_ge(act_fstd, 1)
            v.reciprocal(stat[:, 6:8], stat[:, 4:6]).then_inc(dve_fin, 1)
            v.wait_ge(dve_fin, TC + 2)
            v.wait_ge(gfin_in, 16)
            for tc in range(TC):
                v.scalar_tensor_tensor(out=hres[:, tc, :], in0=hres[:, tc, :], scalar=stat[:, 6 + tc:7 + tc],
                                       in1=gfin[:, :], op0=ALU.mult, op1=ALU.mult).then_inc(dve_out, 1)

        @block.tensor
        def _(pe):
            pe.wait_ge(gp_step, 4)
            pe.wait_ge(vec_in, 16 * 11)
            for c in range(KC):
                last = pe.transpose(ps[:, 7, c * NROW:(c + 1) * NROW], vecs[:, c * P:(c + 1) * P],
                                    ident[0:NROW, 0:NROW])
            last.then_inc(pe_par, 1)
            pe.wait_ge(par_ready, 1)
            for c in range(KC):
                if c >= 4:
                    pe.wait_ge(act_evac, c - 3)
                for tc in range(TC):
                    if c == 0:
                        pe.wait_ge(dve_xn, tc + 1)
                    last = pe.transpose(ps[:, c % 4, tc * P:(tc + 1) * P], xn[:, tc, c * P:(c + 1) * P],
                                        ident[:, :])
                last.then_inc(pe_chunk, 1)

            with loop(ENG.PE, 0, K_SPLIT // SEG) as s:
                for p in range(SEG):
                    pe.wait_ge(mixw_full[p], s * 16 + 16)
                    w = slot_kn(ring, MIX_SLOT + p)
                    for m in (2 * p, 2 * p + 1):
                        pe.wait_ge(act_evac, s * KC + max(KC + m - 3, KC))
                        for k in range(KC):
                            last = pe.matmul(ps[:, m % 4, 0:T], w[:, k, (m % 2) * P:(m % 2 + 1) * P],
                                             actT[:, k, :], start=(k == 0), stop=(k == KC - 1))
                        last.then_inc(pe_chunk, 1)
            pe.wait_ge(lruw_in, 32)
            for m in range(2 * KC):
                c, w = m // 2, m % 2
                if w == 0:
                    pe.wait_ge(dve_conv4, c + 1)
                if m >= 4:
                    pe.wait_ge(act_lru, m - 3)
                pe.matmul(ps[:, 4 + m % 4, 0:T], lruw[:, w, c, :], bufB[:, c, :], start=True, stop=True
                          ).then_inc(pe_lru, 1)

            def split_products(dst, w_hi, w_lo, x_hi, x_lo):
                for k in range(KC):
                    pe.matmul(dst, w_hi(k), x_hi(k), start=(k == 0), stop=False)
                    pe.matmul(dst, w_hi(k), x_lo(k), start=False, stop=False)
                    last = pe.matmul(dst, w_lo(k), x_hi(k), start=False, stop=(k == KC - 1))
                return last

            def split_panel(n, x_hi, x_lo, before):
                pe.wait_ge(dve_wlo, n + 1)
                w_hi, w_lo = slot_kn(ring_r, HI_SLOT + n % SEG), slot_kn(ring_r, MIX_SLOT + n % SEG)
                for m in (2 * n, 2 * n + 1):
                    before(m)
                    cols = slice((m % 2) * P, (m % 2 + 1) * P)
                    split_products(ps[:, m % 4, 0:T], lambda k: w_hi[:, k, cols], lambda k: w_lo[:, k, cols],
                                   lambda k: x_hi[:, k, 0:T], lambda k: x_lo[:, k, 0:T]).then_inc(pe_chunk, 1)

            def channel_sums(src, bank):
                for c in range(KC):
                    last = pe.matmul(ps[:, bank, 0:T], ones[:, :], src[:, c, :], start=(c == 0), stop=(c == KC - 1))
                last.then_inc(pe_sum, 1)

            def evac_bank(m):
                pe.wait_ge(act_evac, KC + 2 * K_SPLIT + m - 3)

            pe.wait_ge(dve_split, 1)
            for n in range(2 * SEG):
                split_panel(n, u_hi, u_lo, evac_bank)
                if n == SEG - 1:
                    pe.wait_ge(dve_conv, KC)
                    channel_sums(cpad[:, :, CONVW - 1:], 4)
                if n == 2 * SEG - 2:
                    pe.wait_ge(act_sq, 1)
                    channel_sums(bufB, 5)
            pe.wait_ge(dve_split, 2)
            for n in range(2 * SEG, 3 * SEG):
                split_panel(n, bufA_r, bufG_r, evac_bank)
            pe.wait_ge(dve_split, 3)

            def yb_bank(m):
                m -= 6 * SEG
                if m < 4:
                    pe.wait_ge(act_evac, 8 * KC + m - 3)
                else:
                    pe.wait_ge(dve_yb, 2 * (m - 3) - 1)
            for n in range(3 * SEG, 4 * SEG):
                split_panel(n, cpad_r, bufC_r, yb_bank)

            def h_transposes(p):
                for c in (2 * p, 2 * p + 1):
                    if c >= 2:
                        pe.wait_ge(act_hT, c - 1)
                    for tc in range(TC):
                        pe.wait_ge(dve_h, 2 * p + tc + 1)
                        last = pe.transpose(ps[:, c % 2, tc * P:(tc + 1) * P], hres[:, tc, c * P:(c + 1) * P],
                                            ident[:, :])
                    last.then_inc(pe_hT, 1)

            def logits(p):
                for c in (2 * p, 2 * p + 1):
                    pe.wait_ge(act_hT, c + 1)
                    for tc in range(TC):
                        last = pe.matmul(ps[:, 2 + tc, 0:NG + NE], actT[:, c, tc * P:(tc + 1) * P], wrt[:, c, :],
                                         start=(c == 0), stop=(c == KC - 1))
                return last

            pe.wait_ge(dve_gw, KC)
            pe.wait_ge(dve_split, 3 + KC)
            for p in range(SEG):
                pe.wait_ge(dve_wlo, 4 * SEG + p + 1)
                w_hi, w_lo = slot_kn(ring_r, HI_SLOT + p), slot_kn(ring_r, MIX_SLOT + p)
                for tc in range(TC):
                    if p:
                        pe.wait_ge(dve_h, 2 * (p - 1) + tc + 1)
                    tok = slice(tc * P, (tc + 1) * P)
                    split_products(ps[:, 4 + tc, 0:PN], lambda k: bufA_r[:, k, tok], lambda k: gateA_r[:, k, tok],
                                   lambda k: w_hi[:, k, :], lambda k: w_lo[:, k, :]).then_inc(pe_wout, 1)
                if p >= 1:
                    h_transposes(p - 1)
                if p >= 2:
                    logits(p - 2)
            h_transposes(SEG - 1)
            logits(SEG - 2)
            logits(SEG - 1).then_inc(pe_logit, 1)
            pe.wait_ge(dve_mask, 1)
            mask = rt[:, 9, :, :]
            pe.matmul(ps[:, 6, 0:NE], tri[:, :], mask[:, 0, :], start=True, stop=True)
            pe.matmul(ps[:, 6, NE:2 * NE], ones[:, :], mask[:, 0, :], start=True, stop=False)
            pe.matmul(ps[:, 6, NE:2 * NE], tri[:, :], mask[:, 1, :], start=False, stop=True)
            pe.matmul(ps[:, 6, 2 * NE:3 * NE], ones[:, :], mask[:, 0, :], start=True, stop=False)
            pe.matmul(ps[:, 6, 2 * NE:3 * NE], ones[:, :], mask[:, 1, :], start=False, stop=True
                      ).then_inc(pe_rank, 1)
            pe.wait_ge(dve_rank, 1)
            for tc in range(TC):
                last = pe.transpose(ps[0:NE, 7, tc * P:(tc + 1) * P], rank[:, tc, 0:NE], ident[:, :])
            last.then_inc(pe_rankT, 1)

            def scatter(pair, stop=False):
                for tc in range(TC):
                    for nn in range(2):
                        for y in (y_hi, y_lo):
                            last = pe.matmul(ps[:, 2 * tc + nn, :], selT[:, pair, tc * P:(tc + 1) * P],
                                             y[:, nn * 512:(nn + 1) * 512],
                                             start=False, stop=stop and y is y_lo, skip_group_check=True)
                last.then_inc(pe_scat, 1)

            pe.wait_ge(gp_step, 12)
            pe.wait_ge(dve_rankT, 1)
            for b in (0, 1, 2, 3, 6, 7):
                last = pe.matmul(ps[:, b, :], selT[:, 0, 0:P], selT[:, :, :].rearrange("p a t -> p (a t)"),
                                 start=True, stop=b >= 6, skip_group_check=True)
            last.then_inc(pe_down, 1)
            pe.wait_ge(dve_hn, TC)
            pe.wait_ge(rounds_ready, 1)
            n_rounds = nc.values_load(rounds[0:1, 0:1], engines=[ENG.PE], min_val=1, max_val=4)
            pe.wait_ge(dve_comb, 1)
            pe.wait_ge(rankq_in, 16 * NQ)
            with loop(ENG.PE, 0, n_rounds * NQ) as g:
                q = g % NQ
                pe.wait_ge(dve_sel, g + 1)
                for c in range(KC):
                    if c >= 2:
                        pe.wait_ge(act_xslot, g * KC + (c - 1))
                    for i, (part, tc) in enumerate([(a, b) for a in (hn_hi, hn_lo) for b in range(TC)]):
                        last = pe.matmul(ps[:, 4 + c % 2, 0:T], part[:, tc, c * P:(c + 1) * P],
                                         sel[:, tc, :], start=(i == 0), stop=(i == 2 * TC - 1))
                    last.then_inc(pe_gather, 1)
                for pair in range(2):
                    for s in range(6 * pair, 6 * pair + 4):
                        pe.wait_ge(ex_full[s], g * 16 + 16)
                    if pair == 0:
                        pe.wait_ge(act_xslot, g * KC + KC)
                    else:
                        pe.wait_ge(act_hidT, g * 2 + 1)
                    for k in range(KC):
                        for j in range(2):
                            s = 6 * pair + 2 * j
                            e = 2 * pair + j
                            w = ring[:, s:s + 2, k * FE:(k + 1) * FE]
                            last = pe.matmul(ps[SLOTS * j:SLOTS * (j + 1), 4, :],
                                             xslot[:, k, e * SLOTS:(e + 1) * SLOTS], w,
                                             start=(k == 0), stop=(k == KC - 1), skip_group_check=True)
                    last.then_inc(pe_gu, 1)
                    pe.wait_ge(dve_ylo, g * 2 + (pair + 1))
                    for tc in range(TC):
                        last = pe.matmul(ps[:, 6, 0:4], sel[:, tc, pair * P:(pair + 1) * P],
                                         comb_hl[:, tc, bass.ds(q * QUAD + 2 * pair, 2), :].rearrange("p a b -> p (a b)"),
                                         start=(tc == 0), stop=(tc == TC - 1))
                    last.then_inc(pe_ws, 1)
                    if pair == 1:
                        pe.wait_ge(dve_selT, g + 1)
                    scatter(1 - pair)
                    if pair == 0:
                        for a in range(2):
                            last = pe.matmul(ps[:, 5, a * T:(a + 1) * T], pair_row[:, a, :],
                                             rank_q[:, bass.ds(q, 1), :].rearrange("e a t -> e (a t)"),
                                             start=True, stop=True)
                        last.then_inc(pe_bc, 1)
                    pe.wait_ge(dve_hid, g * 2 + (pair + 1))
                    for f in range(FC):
                        last = pe.transpose(ps[:, 4, f * P:(f + 1) * P], hid[:, f * P:(f + 1) * P], ident[:, :])
                    last.then_inc(pe_hidT, 1)
                    pe.wait_ge(ex_full[6 * pair + 4], g * 16 + 16)
                    pe.wait_ge(ex_full[6 * pair + 5], g * 16 + 16)
                    pe.wait_ge(act_hidT, g * 2 + (pair + 1))
                    pe.wait_ge(dve_ws, g * 4 + (2 * pair + 3))
                    for nn in range(2):
                        for f in range(FC):
                            for j in range(2):
                                w = ring[:, 6 * pair + 4 + j, :].rearrange("p (f n) -> p f n", f=FC)
                                last = pe.matmul(ps[SLOTS * j:SLOTS * (j + 1), 6 + nn, :],
                                                 hidT[:, f, SLOTS * j:SLOTS * (j + 1)],
                                                 w[:, f, nn * 512:(nn + 1) * 512],
                                                 start=(f == 0), stop=(f == FC - 1), skip_group_check=True)
                    last.then_inc(pe_down, 1)
            pe.wait_ge(dve_ylo, n_rounds * (2 * NQ) + 1)
            scatter(1, stop=True)


_INS = ["x", "g_mix", "w_in", "rnn_conv_w", "rnn_conv_b", "lru_w_r", "lru_b_r", "lru_w_i", "lru_b_i",
        "lru_a_param", "w_rnn_out", "conf_conv_w", "conf_conv_b", "conf_ln_g", "conf_ln_b", "w_conf_out",
        "w_out", "g_ffn", "w_group_router", "b_group_router", "w_expert_router", "b_expert_router",
        "w_gate", "w_up", "w_down", "g_final"]


def kernel(**inputs):
    import numpy as np
    import concourse.bacc as bacc
    from concourse.bass_utils import run_bass_kernel_spmd

    nc = bacc.Bacc("TRN2", target_bir_lowering=False, num_devices=1)
    arrays, args = {}, []
    for name in _INS:
        a = np.ascontiguousarray(inputs[name])
        arrays[f"in_{name}"] = a
        args.append(nc.dram_tensor(f"in_{name}", a.shape, mybir.dt.from_np(a.dtype), kind="ExternalInput").ap())
    shape = inputs["x"].shape
    out = nc.dram_tensor("out", shape, F32, kind="ExternalOutput").ap()
    build(nc, *args, out)
    r = run_bass_kernel_spmd(nc, [arrays], core_ids=[0])
    return r.results[0]["out"]
```

```python
from contextlib import ExitStack

import concourse.bass as bass
from concourse import mybir

F32 = mybir.dt.float32
F32R = mybir.dt.float32r
BF16 = mybir.dt.bfloat16
I32 = mybir.dt.int32
ALU = mybir.AluOpType
ACT = mybir.ActivationFunctionType
ENG = mybir.EngineType
AX = mybir.AxisListType.X

P = 128
T = 256
TC = T // P
D = 1024
KC = D // P
CONVW = 31
RNNW = 4
LRU_C = 8.0
RMS_EPS = 1e-6
LN_EPS = 1e-5
NG = 4
NE = 32
PER_GROUP = NE // NG
FE = 256
FC = FE // P
SLOTS = 64
QUAD = 4
NQ = NE // QUAD
PANEL = 2048
PN = PANEL // KC
SEG = D // PN
NMIX = 9 * SEG
UNITS = 6
RING = 8
SPAN = 4
SPAN_UNITS = SPAN * UNITS
EXTRA = 20
LOW = 6
K_RNN, K_GELU, K_GA, K_GB, K_YA, K_YB, K_WOUT = (n * SEG for n in range(2, 9))
SPLIT = [1, 2, 3] + list(range(K_GA, NMIX))
HI_SLOT, MIX_SLOT = SEG, 2 * SEG

R_GMIX, R_RCB, R_RCW, R_BR, R_BI, R_A, R_CCB, R_LNG, R_LNB, R_GFFN, R_CCW = 0, 1, 2, 6, 7, 8, 9, 10, 11, 12, 13
NROW = R_CCW + CONVW


def bcast(ap, axis, n):
    shape = list(ap.shape)
    shape[axis] = n
    return ap.broadcast_to(shape)


def build(nc, x, g_mix, w_in, rnn_conv_w, rnn_conv_b, lru_w_r, lru_b_r, lru_w_i, lru_b_i, lru_a_param,
          w_rnn_out, conf_conv_w, conf_conv_b, conf_ln_g, conf_ln_b, w_conf_out, w_out, g_ffn,
          w_group_router, b_group_router, w_expert_router, b_expert_router, w_gate, w_up, w_down,
          g_final, out):
    stack = ExitStack()
    mixer_mem = ExitStack()

    def sb(name, shape, dt=F32, where=None):
        return (where or stack).enter_context(nc.sbuf_tensor(name, shape, dt))

    def loop(engine, lo, hi):
        return nc.Fori(lo, hi, engines=(engine,), hint_back_edge=True)

    def sem(name):
        return stack.enter_context(nc.semaphore(name))

    with stack:
        with ExitStack() as alias:
            ring = sb("ring", [P, 2 * LOW, PANEL], F32, alias)
        ring_r = sb("ring_r", [P, 2 * LOW, PANEL], F32R)
        with ExitStack() as alias:
            hres = sb("hres", [P, TC, D], F32, alias)
            actT = sb("actT", [P, KC, T], F32, alias)
        extra = sb("extra", [P, 2, PANEL])
        par = sb("par", [P, KC, NROW])
        ident = sb("ident", [P, P])
        ones = sb("ones", [P, P])
        tri_b = sb("tri_b", [P, P], BF16)
        ones_b = sb("ones_b", [P, P], BF16)
        wrt = sb("wrt", [P, KC, NG + NE])
        brt = sb("brt", [P, NG + NE])
        stat = sb("stat", [P, 20])
        rounds = sb("rounds", [P, 1], I32)
        iota_s = sb("iota_s", [P, SLOTS])
        desc = sb("desc", [P, NE])
        slot_no = sb("slot_no", [P, 1])
        pair_row = sb("pair_row", [QUAD, 2, P], BF16)
        selT = sb("selT", [P, 2, T], F32R)
        wslot = sb("wslot", [P, 2])
        ssp = sb("ssp", [P, TC, SEG])
        u_hi = sb("u_hi", [P, KC, T], F32R, mixer_mem)
        u_lo = sb("u_lo", [P, KC, T], F32R, mixer_mem)
        MIXER = [("bufG", 0), ("cpad", CONVW - 1), ("bufC", 0), ("bufA", RNNW - 1), ("gateA", 0),
                 ("bufB", 0), ("bufD", 0), ("gateB", 0)]
        with ExitStack() as alias:
            bufG, cpad, bufC, bufA, gateA, bufB, bufD, gateB = (
                sb(name, [P, KC, T + pad], F32, alias) for name, pad in MIXER)
        bufG_r, cpad_r, bufC_r, bufA_r, gateA_r, _, _, _ = (
            sb(name + "_r", [P, KC, T + pad], F32R, mixer_mem) for name, pad in MIXER)
        vecs = bufB[0:NROW, 0:4, :].rearrange("p a b -> p (a b)")
        rdiag = bufD[:, 0, :].rearrange("p (t a) -> p t a", t=TC)
        lruw = gateB[:, :, :].rearrange("p (w a) (h j) -> p w (a h) j", w=2, h=2)
        lsc = sb("lsc", [P, 8, KC], F32, mixer_mem)
        cacc = sb("cacc", [P, 2, T], F32, mixer_mem)
        lnw = sb("lnw", [P, 3, T], F32, mixer_mem)
        mixer_mem.close()
        moe_mem = stack
        ring_high = sb("ring_high", [P, 2 * (RING - LOW), PANEL], F32, moe_mem)
        with ExitStack() as alias:
            hg = sb("hg", [P, TC, D], F32, alias)
        xslot = sb("xslot", [P, KC, QUAD * SLOTS], F32, moe_mem)
        hn_hi = sb("hn_hi", [P, TC, D], F32R, moe_mem)
        hn_lo = sb("hn_lo", [P, TC, D], F32R, moe_mem)
        sel = sb("sel", [P, TC, QUAD * SLOTS], F32R, moe_mem)
        gffn = sb("gffn", [P, D], F32, moe_mem)
        gfin = sb("gfin", [P, D], F32, moe_mem)
        y_hi = sb("y_hi", [P, D], F32R, moe_mem)
        y_lo = sb("y_lo", [P, D], F32R, moe_mem)
        sgate = sb("sgate", [P, FE], F32, moe_mem)
        hid = sb("hid", [P, FE], F32, moe_mem)
        hidT = sb("hidT", [P, FC, P], F32, moe_mem)
        logit = sb("logit", [P, TC, NG + NE], F32, moe_mem)
        rt = sb("rt", [P, 12, TC, NE], F32, moe_mem)
        mask = sb("mask", [P, TC, NE], BF16, moe_mem)
        comb_hl = sb("comb_hl", [P, TC, NE, 2], F32R, moe_mem)
        rank = sb("rank", [P, TC, NE + QUAD], F32, moe_mem)
        rank_q = sb("rank_q", [QUAD, NQ, T], BF16, moe_mem)
        rankT = sb("rankT", [NE, T], BF16, moe_mem)
        ps = stack.enter_context(nc.psum_tensor("ps", [P, 8, 512], F32))

        x_in = [sem(f"x_in{tc}") for tc in range(TC)]
        vec_in = sem("vec_in")
        lruw_in = sem("lruw_in")
        router_in = sem("router_in")
        gains_in = sem("gains_in")
        mixw_full = [sem(f"mixw_full{i}") for i in range(SEG)]
        ex_full = [sem(f"ex_full{i}") for i in range(RING)]
        extra_full = sem("extra_full")
        pe_h_in = sem("pe_h_in")
        out_done = sem("out_done")
        gp_step = sem("gp_step")
        dve_step = sem("dve_step")
        dve_rdiag = sem("dve_rdiag")
        pe_rstd = sem("pe_rstd")
        dve_rstd = sem("dve_rstd")
        dve_u = sem("dve_u")
        pe_par = sem("pe_par")
        par_ready = sem("par_ready")
        act_ssq = sem("act_ssq")
        dve_var = sem("dve_var")
        act_std = sem("act_std")
        act_whi = sem("act_whi")
        dve_wlo = sem("dve_wlo")
        act_split = sem("act_split")
        dve_split = sem("dve_split")
        act_lexp = sem("act_lexp")
        act_tap = sem("act_tap")
        act_ctap = sem("act_ctap")
        dve_labs = sem("dve_labs")
        dve_lsc = sem("dve_lsc")
        pe_chunk = sem("pe_chunk")
        act_evac = sem("act_evac")
        dve_conv4 = sem("dve_conv4")
        pe_lru = sem("pe_lru")
        act_lru = sem("act_lru")
        dve_lru = sem("dve_lru")
        dve_cmul = sem("dve_cmul")
        dve_conv = sem("dve_conv")
        pe_sum = sem("pe_sum")
        dve_cent = sem("dve_cent")
        act_sq = sem("act_sq")
        dve_norm = sem("dve_norm")
        act_silu = sem("act_silu")
        dve_yb = sem("dve_yb")
        pe_wout = sem("pe_wout")
        dve_h = sem("dve_h")
        pe_hT = sem("pe_hT")
        act_hT = sem("act_hT")
        dve_gw = sem("dve_gw")
        pe_logit = sem("pe_logit")
        dve_rstd2 = sem("dve_rstd2")
        dve_hg = sem("dve_hg")
        act_hn = sem("act_hn")
        dve_hn = sem("dve_hn")
        dve_route = sem("dve_route")
        act_rexp = sem("act_rexp")
        pe_rank = sem("pe_rank")
        dve_mask = sem("dve_mask")
        dve_rank = sem("dve_rank")
        pe_rankT = sem("pe_rankT")
        dve_comb = sem("dve_comb")
        dve_rankT = sem("dve_rankT")
        rounds_ready = sem("rounds_ready")
        rankq_in = sem("rankq_in")
        pe_scat = sem("pe_scat")
        dve_sel = sem("dve_sel")
        pe_gather = sem("pe_gather")
        act_xslot = sem("act_xslot")
        pe_bc = sem("pe_bc")
        dve_selT = sem("dve_selT")
        pe_gu_half = sem("pe_gu_half")
        pe_gu = sem("pe_gu")
        act_sg = sem("act_sg")
        dve_hid = sem("dve_hid")
        pe_ws = sem("pe_ws")
        dve_ws = sem("dve_ws")
        pe_hidT = sem("pe_hidT")
        act_hidT = sem("act_hidT")
        pe_down = sem("pe_down")
        pe_down_half = sem("pe_down_half")
        act_yhi = sem("act_yhi")
        dve_ylo = sem("dve_ylo")
        dve_fin = sem("dve_fin")
        act_fssq = sem("act_fssq")
        act_fstd = sem("act_fstd")
        dve_out = sem("dve_out")

        x_v = x.rearrange("b (t p) d -> p (b t) d", p=P)
        out_v = out.rearrange("b (t p) d -> p (b t) d", p=P)

        def rows_by_chunk(w):
            return w.rearrange("(k p) n -> p k n", p=P)

        win_v = rows_by_chunk(w_in[0])
        tail_v = [rows_by_chunk(w[0]) for w in (w_rnn_out, w_conf_out, w_out)]
        SEG_RNN, SEG_GELU, SEG_CVAL, SEG_CGATE, SEG_GA, SEG_GB = range(6)

        C_HALVES = (slice(0, KC // 2), slice(KC // 2, KC))

        def unit(u):
            return ring[:, 2 * u:2 * u + 2, :] if u < LOW else ring_high[:, 2 * (u - LOW):2 * (u - LOW) + 2, :]

        def slot_kn(t, s):
            return t[:, s, :].rearrange("p (k n) -> p k n", k=KC)

        param_rows = [(R_GMIX, g_mix), (R_CCW, conf_conv_w[0]), (R_RCW, rnn_conv_w[0]), (R_RCB, rnn_conv_b),
                      (R_CCB, conf_conv_b), (R_GFFN, g_ffn),
                      (R_BR, lru_b_r.rearrange("l h j -> l (h j)")),
                      (R_BI, lru_b_i.rearrange("l h j -> l (h j)")), (R_A, lru_a_param),
                      (R_LNG, conf_ln_g), (R_LNB, conf_ln_b)]

        block = stack.enter_context(nc.Block())

        @block.sync
        def _(sp):
            for tc in range(TC):
                sp.dma_start(hres[:, tc, :], x_v[:, tc, :]).then_inc(x_in[tc], 16)
            for r, v in param_rows[:5]:
                sp.dma_start(vecs[r:r + v.shape[0], :], v).then_inc(vec_in, 16)

            def load_unit(g, n):
                pair, part = n % UNITS // 3, n % 3
                dst, full = (extra[:, :, :], extra_full) if n == EXTRA else (unit(n % RING), ex_full[n % RING])
                for j in range(2):
                    e = g % NQ * QUAD + (2 * pair + j)
                    for h in range(2):
                        if part < 2:
                            src = (w_gate, w_up)[h][0, bass.ds(e, 1), :, :].rearrange("a (k p) n -> p (a k) n", p=P)
                            src = src[:, part * KC // 2:(part + 1) * KC // 2, :]
                            d = dst.rearrange("p a (k n) -> p (a k) n", n=4 * FE)
                            d = d[:, :, (2 * j + h) * FE:(2 * j + h + 1) * FE]
                        else:
                            src = w_down[0, bass.ds(e, 1), :, :].rearrange("a (f p) n -> p (a f) n", p=P)[:, h, :]
                            d = dst[:, j, h * D:(h + 1) * D]
                        sp.dma_start(d, src).then_inc(full, 16)

            def place_free(first, n):
                if n % SPAN_UNITS == (EXTRA + RING) % SPAN_UNITS:
                    return
                before = n - (SPAN_UNITS if n == EXTRA else RING)
                g, pair, part = first + before // UNITS, before % UNITS // 3, before % 3
                if part < 2:
                    sp.wait_ge((pe_gu_half, pe_gu)[part], g * 2 + (pair + 1))
                else:
                    sp.wait_ge(pe_down, g * 2 + (pair + 2))

            order = [(seg, p) for p in range(SEG) for seg in (SEG_CVAL, SEG_CGATE)]
            order += [(seg, p) for seg in (SEG_RNN, SEG_GELU, SEG_GA, SEG_GB, 6, 7, 8) for p in range(SEG)]
            for k in range(NMIX):
                if k >= SEG:
                    sp.wait_ge(pe_chunk, KC + 2 * (k - SEG + 1))
                seg, p = order[k]
                if seg < 6:
                    src = win_v[:, :, seg * D + p * PN: seg * D + (p + 1) * PN]
                else:
                    src = tail_v[seg - 6][:, :, p * PN:(p + 1) * PN]
                sp.dma_start(slot_kn(ring, MIX_SLOT + k % SEG), src).then_inc(mixw_full[k % SEG], 16)
                if k in (K_RNN, K_RNN + SEG // 2):
                    load_unit(0, (k - K_RNN) // 2)
                if k == K_YB + 1:
                    load_unit(LOW // UNITS, LOW)
            sp.wait_ge(pe_chunk, KC + 8 * KC)
            sp.wait_ge(dve_yb, 1)
            sp.dma_start(gffn[:, :], bcast(g_ffn, 0, P)).then_inc(gains_in, 16)
            sp.dma_start(gfin[:, :], bcast(g_final.rearrange("(a d) -> a d", a=1), 0, P)).then_inc(gains_in, 16)
            load_unit((LOW + 1) // UNITS, LOW + 1)
            for p in (1, 3):
                sp.wait_ge(pe_wout, 2 * (p + 1))
                for s in (HI_SLOT + p, MIX_SLOT + p):
                    load_unit(0, s // 2)
            sp.wait_ge(pe_h_in, 1)
            load_unit(EXTRA // UNITS, EXTRA)
            sp.wait_ge(dve_rankT, 1)
            for q in range(NQ):
                sp.dma_start(rank_q[:, q, :], rankT[q * QUAD:(q + 1) * QUAD, :]).then_inc(rankq_in, 16)
            for n in range(RING, SPAN_UNITS):
                if n != EXTRA:
                    place_free(0, n)
                    load_unit(n // UNITS, n)
            sp.wait_ge(rounds_ready, 1)
            n_rounds = nc.values_load(rounds[0:1, 0:1], engines=[ENG.SP], min_val=1, max_val=4)
            with loop(ENG.SP, 1, n_rounds * (NQ // SPAN)) as i:
                for n in range(SPAN_UNITS):
                    place_free(i * SPAN, n)
                    load_unit(i * SPAN + n // UNITS, n)
            for tc in range(TC):
                for half in range(2):
                    cols = slice(half * D // 2, (half + 1) * D // 2)
                    sp.wait_ge(dve_out, 2 * tc + half + 1)
                    sp.dma_start(out_v[:, tc, cols], hres[:, tc, cols]).then_inc(out_done, 16)
            sp.wait_ge(out_done, 16 * 2 * TC)

        @block.gpsimd
        def _(gp):
            n = [0]

            def link(ins):
                n[0] += 1
                ins.then_inc(gp_step, 1)
                gp.wait_ge(gp_step, n[0])

            link(gp.memset(ident[:, :], 0.0))
            link(gp.memset(ones[:, :], 1.0))
            link(gp.affine_select(out=ident[:, :], in_=ident[:, :], compare_op=ALU.not_equal, fill=1.0, base=0,
                                  pattern=[[-1, P]], channel_multiplier=1))
            link(gp.memset(ones_b[:, :], 1.0))
            link(gp.affine_select(out=tri_b[:, :], in_=ones_b[:, :], compare_op=ALU.is_gt, fill=0.0, base=0,
                                  pattern=[[1, P]], channel_multiplier=-1))
            link(gp.memset(bufA[:, :, 0:RNNW - 1], 0.0))
            link(gp.memset(cpad[:, :, 0:CONVW - 1], 0.0))
            link(gp.iota(iota_s[:, :], pattern=[[1, SLOTS]], base=1, channel_multiplier=0,
                         allow_small_or_imprecise_dtypes=True))
            link(gp.iota(desc[:, :], pattern=[[-1, NE]], base=NE, channel_multiplier=0,
                         allow_small_or_imprecise_dtypes=True))
            for half in (slice(0, SLOTS), slice(SLOTS, P)):
                link(gp.iota(slot_no[half, :], pattern=[[0, 1]], base=1, channel_multiplier=1,
                             allow_small_or_imprecise_dtypes=True))
            link(gp.tensor_scalar(selT[:, :, :].rearrange("p a (b t) -> p (a b) t", b=TC),
                                  bcast(ones[:, :].rearrange("p (a t) -> p a t", a=1), 1, 2 * TC),
                                  0.0, None, ALU.mult))
            gp.memset(wslot[:, :], 0.0).then_inc(dve_ws, 1)
            gp.wait_ge(dve_ws, 1)
            link(gp.memset(pair_row[:, :, :], 0.0))
            link(gp.affine_select(out=pair_row[:, :, :].rearrange("q a (b s) -> q (a b) s", b=2),
                                  in_=pair_row[:, :, :].rearrange("q a (b s) -> q (a b) s", b=2),
                                  compare_op=ALU.not_equal, fill=1.0, base=0,
                                  pattern=[[-1, QUAD], [0, SLOTS]], channel_multiplier=1))
            gp.wait_ge(mixw_full[SEG - 1], 16)
            gp.dma_start(lruw[:, 0, :, :], lru_w_r[0].rearrange("h i j -> i h j")).then_inc(lruw_in, 16)
            gp.dma_start(lruw[:, 1, :, :], lru_w_i[0].rearrange("h i j -> i h j")).then_inc(lruw_in, 16)
            gp.dma_start(wrt[:, :, 0:NG], rows_by_chunk(w_group_router[0])).then_inc(router_in, 16)
            gp.dma_start(wrt[:, :, NG:], rows_by_chunk(w_expert_router[0])).then_inc(router_in, 16)
            gp.dma_start(brt[:, 0:NG], bcast(b_group_router, 0, P)).then_inc(router_in, 16)
            gp.dma_start(brt[:, NG:], bcast(b_expert_router, 0, P)).then_inc(router_in, 16)

        @block.scalar
        def _(act):
            for r, v in param_rows[5:]:
                act.dma_start(vecs[r:r + v.shape[0], :], v).then_inc(vec_in, 16)

            def ready(func, n):
                act.activation(stat[:, 16 + n:17 + n], ones[:, 0:1], func)

            act.wait_ge(gp_step, 2)
            ready(ACT.Sqrt, 0)
            for tc in range(TC):
                act.wait_ge(x_in[tc], 16)
                act.activation(gateA[:, 4 * tc:4 * tc + 4, :].rearrange("p a b -> p (a b)"), hres[:, tc, :], ACT.Square,
                               accum_out=stat[:, tc:tc + 1]).then_inc(act_ssq, 1)
            act.wait_ge(dve_var, 1)
            act.activation(stat[:, 4:6], stat[:, 2:4], ACT.Sqrt).then_inc(act_std, 1)
            act.wait_ge(pe_chunk, KC)
            act.wait_ge(par_ready, 1)
            for c in range(KC):
                act.activation(actT[:, c, :], ps[:, c % 4, c // 4 * T:(c // 4 + 1) * T], ACT.Copy,
                               scale=par[:, c, R_GMIX:R_GMIX + 1]).then_inc(act_evac, 1)

            def take_conformer(i):
                for b in range(4):
                    act.wait_ge(pe_chunk, i * 4 + (KC + b + 1))
                    c = bass.ds(i * 2 + b % 2, 1)
                    d = cpad[:, c, CONVW - 1:] if b < 2 else gateA[:, c, :]
                    act.activation(d.rearrange("p a b -> p (a b)"), ps[:, b, 0:T],
                                   ACT.Copy if b < 2 else ACT.Sigmoid).then_inc(act_evac, 1)

            def weight_hi(k):
                act.wait_ge(mixw_full[k % SEG], 16 * (k // SEG + 1))
                act.activation(ring_r[:, HI_SLOT + k % SEG, :], ring[:, MIX_SLOT + k % SEG, :], ACT.Copy
                               ).then_inc(act_whi, 1)

            def take_panel(k, func, dst, before=None):
                for m in (2 * k, 2 * k + 1):
                    c = m % KC
                    act.wait_ge(pe_chunk, KC + m + 1)
                    if before:
                        before(c)
                    act.activation(dst[:, c, 0:T], ps[:, m % 4, 0:T], func).then_inc(act_evac, 1)

            def take_ga(p):
                take_panel(K_GA + p, ACT.Sigmoid, gateA, before=lambda c: act.wait_ge(dve_cmul, c + 1))

            def take_gb(p):
                take_panel(K_GB + p, ACT.Sigmoid, gateB)

            def take_ya(p):
                take_panel(K_YA + p, ACT.Copy, bufD)

            act.wait_ge(dve_u, KC)
            act.activation(u_hi[:, :, :], actT[:, :, :], ACT.Copy).then_inc(act_split, 1)
            for k in SPLIT[:3]:
                weight_hi(k)
            act.wait_ge(dve_labs, 1)
            act.activation(lsc[:, 1, :], lsc[:, 0, :], ACT.Exp, scale=-1.0).then_inc(act_lexp, 1)
            ready(ACT.Sigmoid, 3)
            def first_taps(i):
                act.wait_ge(dve_cmul, i * 2 + 2)
                for c in (2 * i, 2 * i + 1):
                    act.activation(bufC[:, c, :], cpad[:, c, 0:T], ACT.Identity, scale=par[:, c, R_CCW:R_CCW + 1],
                                   bias=par[:, c, R_CCB:R_CCB + 1]).then_inc(act_ctap, 1)

            def take_rnn(i):
                for b in range(4):
                    c = i * 4 + b
                    act.wait_ge(pe_chunk, 3 * KC + c + 1)
                    act.activation(bufA[:, c, RNNW - 1:], ps[:, b, 0:T], ACT.Copy).then_inc(act_evac, 1)
                    act.wait_ge(act_evac, 3 * KC + c + 1)
                    act.activation(bufB[:, c, :], bufA[:, c, 0:T], ACT.Identity, scale=par[:, c, R_RCW:R_RCW + 1],
                                   bias=par[:, c, R_RCB:R_RCB + 1]).then_inc(act_tap, 1)

            act.wait_ge(gp_step, 7)
            take_conformer(0)
            first_taps(0)
            with loop(ENG.Activation, 1, SEG - 1) as i:
                take_conformer(i)
            first_taps(1)
            take_conformer(SEG - 1)
            first_taps(2)
            take_rnn(0)
            take_rnn(1)
            for p in range(SEG):
                if p >= 2:
                    weight_hi(K_GA + p - 2)
                take_panel(K_GELU + p, ACT.Gelu_apprx_tanh, bufG)
            weight_hi(K_GA + 2)
            take_ga(0)
            for m in range(2 * KC):
                c, w = m // 2, m % 2
                act.wait_ge(pe_lru, m + 1)
                row = (R_BR, R_BI)[w]
                act.activation((bufC, bufD)[w][:, c, :], ps[:, 4 + m % 4, 0:T], ACT.Sigmoid,
                               bias=par[:, c, row:row + 1]).then_inc(act_lru, 1)
            weight_hi(K_GA + 3)
            act.wait_ge(dve_lsc, 1)
            act.wait_ge(act_lru, 2 * KC)
            act.wait_ge(dve_conv4, KC)
            for c in range(KC):
                act.activation(bufA[:, c, 0:T], bufC[:, c, :], ACT.Tanh, scale=lsc[:, 7, c:c + 1]
                               ).then_inc(act_lru, 1)
            weight_hi(K_GA + 4)
            take_ga(1)
            for c in range(KC):
                act.wait_ge(act_lru, 2 * KC + c + 1)
                act.activation(bufC[:, c, :], bufC[:, c, :], ACT.Exp, scale=lsc[:, 7, c:c + 1]
                               ).then_inc(act_lru, 1)
            weight_hi(K_GA + 5)
            take_ga(2)
            weight_hi(K_GA + 6)
            take_ga(3)
            act.wait_ge(dve_lru, 1)
            act.wait_ge(act_lru, 4 * KC)
            act.activation(bufB[:, :, :], bufC[:, :, :], ACT.Square).then_inc(act_lru, 1)
            act.wait_ge(dve_lru, 2)
            act.activation(bufA[:, :, 0:T], bufB[:, :, :], ACT.Sqrt, scale=-1.0).then_inc(act_lru, 1)
            weight_hi(K_GA + 7)
            take_gb(0)
            take_gb(1)
            weight_hi(K_GA + 8)
            weight_hi(K_GA + 9)
            act.wait_ge(dve_lru, 4)
            act.activation(bufA_r[:, :, 0:T], bufG[:, :, :], ACT.Copy).then_inc(act_split, 1)
            take_gb(2)
            act.wait_ge(dve_cent, 1)
            act.activation(bufB[:, :, :], cpad[:, :, CONVW - 1:], ACT.Square).then_inc(act_sq, 1)
            weight_hi(K_GA + 10)
            act.wait_ge(dve_cent, 2)
            act.activation(lnw[:, 2, :], lnw[:, 1, :], ACT.Sqrt).then_inc(act_sq, 1)
            take_gb(3)
            take_ya(0)
            act.wait_ge(dve_norm, 1)
            for c in range(KC):
                act.activation(bufC[:, c, :], cpad[:, c, CONVW - 1:], ACT.Silu, scale=par[:, c, R_LNG:R_LNG + 1],
                               bias=par[:, c, R_LNB:R_LNB + 1]).then_inc(act_silu, 1)
            act.wait_ge(act_silu, KC)
            for half in C_HALVES:
                act.activation(cpad_r[:, half, 0:T], bufC[:, half, :], ACT.Copy).then_inc(act_split, 1)
            weight_hi(K_GA + 11)
            take_ya(1)
            weight_hi(K_GA + 12)
            take_ya(2)
            weight_hi(K_GA + 13)
            take_ya(3)
            for p in range(SEG):
                weight_hi(K_YB + 2 + p)
                for c in (2 * p, 2 * p + 1):
                    act.wait_ge(dve_yb, 2 * c + 2)
                    act.activation(bufA_r[:, c, 0:T], gateA[:, c, :], ACT.Copy).then_inc(act_split, 1)
            weight_hi(K_WOUT + 2)
            weight_hi(K_WOUT + 3)

            def squares(p):
                for tc in range(TC):
                    act.wait_ge(dve_h, 2 * p + tc + 1)
                    act.activation(gateB[:, 2 * p + tc, :], hres[:, tc, p * PN:(p + 1) * PN], ACT.Square,
                                   accum_out=ssp[:, tc, p:p + 1]).then_inc(act_ssq, 1)

            def take_hT(p):
                for c in (2 * p, 2 * p + 1):
                    act.wait_ge(pe_hT, c + 1)
                    act.activation(actT[:, c, :], ps[:, c % 2, 0:T], ACT.Copy).then_inc(act_hT, 1)

            ready(ACT.Sqrt, 1)
            for p in range(SEG):
                squares(p)
                if p:
                    take_hT(p - 1)
            act.wait_ge(dve_var, 2)
            act.activation(stat[:, 4:6], stat[:, 2:4], ACT.Sqrt).then_inc(act_std, 1)
            take_hT(SEG - 1)
            act.wait_ge(dve_rstd2, 1)
            act.wait_ge(dve_hg, 2 * SEG)
            for tc in range(TC):
                act.activation(hn_hi[:, tc, :], hg[:, tc, :], ACT.Copy, scale=stat[:, 6 + tc:7 + tc]
                               ).then_inc(act_hn, 1)
            act.wait_ge(dve_route, 1)
            act.activation(rt[:, 1, :, 0:NG], rt[:, 0, :, 0:NG], ACT.Exp).then_inc(act_rexp, 1)
            act.wait_ge(dve_route, 2)
            act.activation(stat[:, 2:4], stat[:, 8:10], ACT.Exp).then_inc(act_rexp, 1)

            act.wait_ge(rounds_ready, 1)
            n_rounds = nc.values_load(rounds[0:1, 0:1], engines=[ENG.Activation],
                                      min_val=1, max_val=4)

            def weighted_hi(pair, downs, weights):
                act.wait_ge(pe_down, downs)
                act.wait_ge(dve_ws, weights)
                act.activation(y_hi[:, :], ps[:, 6:8, :].rearrange("p a b -> p (a b)"), ACT.Copy,
                               scale=wslot[:, pair:pair + 1]).then_inc(act_yhi, 1)

            act.wait_ge(dve_rankT, 1)
            with loop(ENG.Activation, 0, n_rounds * NQ) as g:
                for c in range(KC // 2):
                    act.wait_ge(pe_gather, g * (KC // 2) + (c + 1))
                    if c % 2:
                        act.wait_ge(dve_hn, TC + (c + 1) // 2)
                    act.activation(xslot[:, 2 * c:2 * c + 2, :].rearrange("p a b -> p (a b)"), ps[:, 4 + c % 2, :],
                                   ACT.Copy).then_inc(act_xslot, 1)
                weighted_hi(1, g * 2 + 1, g * 4 + 1)
                for pair in range(2):
                    act.wait_ge(pe_gu, g * 2 + (pair + 1))
                    act.activation(sgate[:, :], ps[:, 4, 0:FE], ACT.Silu).then_inc(act_sg, 1)
                    act.wait_ge(pe_hidT, g * 2 + (pair + 1))
                    act.activation(hidT[:, :, :].rearrange("p a b -> p (a b)"), ps[:, 4, 0:FE], ACT.Copy
                                   ).then_inc(act_hidT, 1)
                    if pair == 0:
                        weighted_hi(0, g * 2 + 2, g * 4 + 3)
            act.wait_ge(dve_ws, n_rounds * (4 * NQ) + 1)
            for half in range(2):
                act.wait_ge((pe_down_half, pe_down)[half], n_rounds * (2 * NQ) + half)
                act.activation(y_hi[:, half * 512:(half + 1) * 512], ps[:, 6 + half, :], ACT.Copy,
                               scale=wslot[:, 1:2]).then_inc(act_yhi, 1)
            ready(ACT.Sqrt, 2)
            act.wait_ge(pe_scat, n_rounds * (4 * NQ) + 4)
            for tc in range(TC):
                act.activation(xslot[:, 4 * tc:4 * tc + 4, :].rearrange("p a b -> p (a b)"),
                               ps[:, 2 * tc:2 * tc + 2, :].rearrange("p a b -> p (a b)"), ACT.Square,
                               accum_out=stat[:, tc:tc + 1]).then_inc(act_fssq, 1)
                act.wait_ge(dve_fin, 2 * tc + 1)
                act.activation(stat[:, 4 + tc:5 + tc], stat[:, 2 + tc:3 + tc], ACT.Sqrt).then_inc(act_fstd, 1)

        @block.vector
        def _(v):
            n = [0]

            def step(ins):
                n[0] += 1
                ins.then_inc(dve_step, 1)
                return n[0]

            def link(ins):
                v.wait_ge(dve_step, step(ins))

            def weight_lo(k):
                v.wait_ge(act_whi, SPLIT.index(k) + 1)
                v.tensor_tensor(ring_r[:, MIX_SLOT + k % SEG, :], ring[:, MIX_SLOT + k % SEG, :],
                                ring_r[:, HI_SLOT + k % SEG, :].bitcast(F32), ALU.subtract).then_inc(dve_wlo, 1)

            def operand_lo(count, lo, full, hi):
                v.wait_ge(act_split, count)
                v.tensor_tensor(lo, full, hi.bitcast(F32), ALU.subtract).then_inc(dve_split, 1)

            v.wait_ge(act_ssq, TC)
            v.tensor_scalar(stat[:, 2:4], stat[:, 0:2], 1.0 / D, RMS_EPS, ALU.mult, ALU.add
                            ).then_inc(dve_var, 1)
            v.wait_ge(pe_par, 1)
            v.tensor_copy(par[:, :, :].rearrange("p k r -> p (k r)"), ps[:, 7, 0:KC * NROW]).then_inc(par_ready, 1)
            v.wait_ge(act_std, 1)
            link(v.reciprocal(stat[:, 6:8], stat[:, 4:6]))
            v.wait_ge(gp_step, 3)
            for tc in range(TC):
                v.tensor_scalar(rdiag[:, tc, :], ident[:, :], stat[:, 6 + tc:7 + tc], None, ALU.mult
                                ).then_inc(dve_rdiag, 1)
            v.wait_ge(pe_rstd, 1)
            v.tensor_copy(lnw[:, 2, :], ps[:, 6, 0:T]).then_inc(dve_rstd, 1)
            v.wait_ge(dve_rstd, 1)
            for c in range(KC):
                v.wait_ge(act_evac, c + 1)
                v.tensor_tensor(actT[:, c, :], actT[:, c, :], lnw[:, 2, :], ALU.mult).then_inc(dve_u, 1)
            v.wait_ge(par_ready, 1)
            a_par = par[:, :, R_A:R_A + 1].rearrange("p k r -> p (k r)")
            link(v.tensor_scalar(lsc[:, 2, :], a_par, -1.0, None, ALU.mult))
            v.tensor_tensor(lsc[:, 0, :], lsc[:, 2, :], a_par, ALU.max).then_inc(dve_labs, 1)
            v.wait_ge(dve_u, KC)
            operand_lo(1, u_lo[:, :, :], actT[:, :, :], u_hi[:, :, :])
            for k in SPLIT[:3]:
                weight_lo(k)
            v.wait_ge(act_lexp, 1)
            link(v.tensor_scalar(lsc[:, 2, :], lsc[:, 1, :], 2.0, None, ALU.add))
            link(v.reciprocal(lsc[:, 3, :], lsc[:, 2, :]))
            link(v.tensor_tensor(lsc[:, 4, :], lsc[:, 1, :], lsc[:, 3, :], ALU.mult))
            link(v.tensor_tensor(lsc[:, 5, :], lsc[:, 4, :], lsc[:, 4, :], ALU.mult))
            link(v.tensor_scalar(lsc[:, 6, :], lsc[:, 5, :], 1.0 / 19, None, ALU.mult))
            for odd in (17, 15, 13, 11, 9, 7, 5, 3):
                link(v.scalar_tensor_tensor(out=lsc[:, 6, :], in0=lsc[:, 6, :], scalar=1.0 / odd,
                                            in1=lsc[:, 5, :], op0=ALU.add, op1=ALU.mult))
            link(v.scalar_tensor_tensor(out=lsc[:, 6, :], in0=lsc[:, 6, :], scalar=1.0,
                                        in1=lsc[:, 4, :], op0=ALU.add, op1=ALU.mult))
            link(v.tensor_scalar(lsc[:, 3, :], a_par, 0.0, LRU_C, ALU.min, ALU.mult))
            v.scalar_tensor_tensor(out=lsc[:, 7, :], in0=lsc[:, 6, :], scalar=-2.0 * LRU_C,
                                   in1=lsc[:, 3, :], op0=ALU.mult, op1=ALU.add).then_inc(dve_lsc, 1)

            def conv(lo, hi, src, acc, dst, taps, w_row, b_row, before, done, between={}, first=0, start=None):
                per = 2 * (taps - 1 - first)
                base = n[0] - lo * per
                with loop(ENG.DVE, lo, hi) as i:
                    before(i)
                    for k in range(first, taps):
                        if k in between:
                            between[k](i)
                        for j in range(2):
                            c = bass.ds(i * 2 + j, 1)
                            s = src[:, c, k:k + T].rearrange("p a b -> p (a b)")
                            a, d = (x(c, j).rearrange("p a b -> p (a b)") for x in (acc, dst))
                            w = par[:, c, w_row + k:w_row + k + 1].rearrange("p a b -> p (a b)")
                            if k == 0:
                                b = par[:, c, b_row:b_row + 1].rearrange("p a b -> p (a b)")
                                ins = v.tensor_scalar(a, s, w, b, ALU.mult, ALU.add)
                            else:
                                if k > first:
                                    v.wait_ge(dve_step, i * per + (base + 2 * (k - 1 - first) + j + 1))
                                sofar = start(c) if start and k == first else a
                                ins = v.scalar_tensor_tensor(out=d if k == taps - 1 else a, in0=s, scalar=w,
                                                             in1=sofar, op0=ALU.mult, op1=ALU.add)
                            ins.then_inc(done if k == taps - 1 else dve_step, 1)
                n[0] += per * (hi - lo)

            def gated(i):
                v.wait_ge(act_evac, i * 4 + (KC + 4))
                for j in range(2):
                    cc = bass.ds(i * 2 + j, 1)
                    c = cpad[:, cc, CONVW - 1:].rearrange("p a b -> p (a b)")
                    v.tensor_tensor(c, c, gateA[:, cc, :].rearrange("p a b -> p (a b)"), ALU.mult
                                    ).then_inc(dve_cmul, 1)

            def conformer_conv(lo, hi, before, **how):
                conv(lo, hi, cpad, lambda c, j: cacc[:, j:j + 1, :], lambda c, j: cpad[:, c, CONVW - 1:],
                     CONVW, R_CCW, R_CCB, before, dve_conv, **how)

            v.wait_ge(gp_step, 14)
            gated(0)
            how = dict(first=1, start=lambda c: bufC[:, c, :].rearrange("p a b -> p (a b)"),
                       between={20: lambda i: gated(i + 1)})
            conformer_conv(0, 1, lambda i: v.wait_ge(act_ctap, 2), **how)

            def tap_and_sums(i):
                v.wait_ge(act_ctap, i * 2 + 2)
                v.wait_ge(dve_conv, i * 2)

            conformer_conv(1, 3, tap_and_sums, **how)
            conv(0, KC // 2, bufA, lambda c, j: bufB[:, c, :], lambda c, j: bufB[:, c, :], RNNW, R_RCW, R_RCB,
                 lambda i: v.wait_ge(act_tap, i * 2 + 2), dve_conv4, first=1)
            weight_lo(K_GA + 0)
            weight_lo(K_GA + 1)

            def input_and_sums(i):
                v.wait_ge(dve_cmul, KC)
                v.wait_ge(dve_conv, KC - 2)

            conformer_conv(3, 4, input_and_sums,
                           between={5: lambda i: weight_lo(K_GA + 2), 18: lambda i: weight_lo(K_GA + 3),
                                    24: lambda i: weight_lo(K_GA + 4)})
            v.wait_ge(act_lru, 2 * KC)
            v.wait_ge(dve_conv4, KC)
            v.tensor_tensor(bufD[:, :, :], bufD[:, :, :], bufB[:, :, :], ALU.mult).then_inc(dve_lru, 1)
            weight_lo(K_GA + 5)
            v.wait_ge(act_lru, 4 * KC + 1)
            v.scalar_tensor_tensor(out=bufB[:, :, :], in0=bufB[:, :, :], scalar=1.0, in1=bufA[:, :, 0:T],
                                   op0=ALU.add, op1=ALU.mult).then_inc(dve_lru, 1)
            weight_lo(K_GA + 6)
            v.wait_ge(act_lru, 4 * KC + 2)
            v.tensor_tensor(bufD[:, :, :], bufD[:, :, :], bufA[:, :, 0:T], ALU.mult).then_inc(dve_lru, 1)
            v.wait_ge(dve_lru, 3)
            for c in range(KC):
                last = step(v.tensor_tensor_scan(bufB[:, c, :], bufC[:, c, :], bufD[:, c, :], 0.0,
                                                 ALU.mult, ALU.add))
            weight_lo(K_GA + 7)
            v.wait_ge(dve_step, last)
            v.wait_ge(act_evac, 5 * KC)
            v.tensor_tensor(bufG[:, :, :], bufG[:, :, :], bufB[:, :, :], ALU.mult).then_inc(dve_lru, 1)
            centred = cpad[:, :, CONVW - 1:]
            v.wait_ge(pe_sum, 1)
            link(v.tensor_scalar(lnw[:, 0, :], ps[:, 4, 0:T], 1.0 / D, None, ALU.mult))
            v.tensor_tensor(centred, centred, bcast(lnw[:, 0:1, :], 1, KC), ALU.subtract).then_inc(dve_cent, 1)
            operand_lo(2, bufG_r[:, :, :], bufG[:, :, :], bufA_r[:, :, 0:T])
            weight_lo(K_GA + 8)
            weight_lo(K_GA + 9)
            v.wait_ge(pe_sum, 2)
            v.tensor_scalar(lnw[:, 1, :], ps[:, 5, 0:T], 1.0 / D, LN_EPS, ALU.mult, ALU.add).then_inc(dve_cent, 1)
            v.wait_ge(act_sq, 2)
            link(v.reciprocal(lnw[:, 0, :], lnw[:, 2, :]))
            v.tensor_tensor(centred, centred, bcast(lnw[:, 0:1, :], 1, KC), ALU.mult).then_inc(dve_norm, 1)
            weight_lo(K_GA + 10)
            for h, half in enumerate(C_HALVES):
                operand_lo(3 + h, bufC_r[:, half, :], bufC[:, half, :], cpad_r[:, half, 0:T])
            weight_lo(K_GA + 11)
            weight_lo(K_GA + 12)
            weight_lo(K_GA + 13)
            v.wait_ge(act_evac, 8 * KC)
            link(v.tensor_tensor(gateA[:, :, :], gateA[:, :, :], bufD[:, :, :], ALU.mult))
            for p in range(SEG):
                for c in (2 * p, 2 * p + 1):
                    v.wait_ge(pe_chunk, KC + 7 * KC + c + 1)
                    v.tensor_tensor(gateB[:, c, :], gateB[:, c, :], ps[:, c % 4, 0:T], ALU.mult).then_inc(dve_yb, 1)
                    v.wait_ge(dve_yb, 2 * c + 1)
                    v.tensor_tensor(gateA[:, c, :], gateA[:, c, :], gateB[:, c, :], ALU.add).then_inc(dve_yb, 1)
                for c in (2 * p, 2 * p + 1):
                    operand_lo(5 + c, gateA_r[:, c, :], gateA[:, c, :], bufA_r[:, c, 0:T])
                weight_lo(K_YB + 2 + p)
            weight_lo(K_WOUT + 2)
            for p in range(SEG):
                for tc in range(TC):
                    v.wait_ge(pe_wout, 2 * p + tc + 1)
                    hcol = hres[:, tc, p * PN:(p + 1) * PN]
                    v.tensor_tensor(hcol, hcol, ps[:, 4 + tc, 0:PN], ALU.add).then_inc(dve_h, 1)
                if p == 0:
                    weight_lo(K_WOUT + 3)
                    v.wait_ge(gains_in, 32)
                if p == 1:
                    v.wait_ge(router_in, 64)
                    for c in range(KC):
                        v.tensor_scalar(wrt[:, c, :], wrt[:, c, :], par[:, c, R_GFFN:R_GFFN + 1], None, ALU.mult
                                        ).then_inc(dve_gw, 1)
                for tc in range(TC):
                    v.wait_ge(dve_h, 2 * p + tc + 1)
                    cols = slice(p * PN, (p + 1) * PN)
                    v.tensor_tensor(hg[:, tc, cols], hres[:, tc, cols], gffn[:, cols], ALU.mult).then_inc(dve_hg, 1)
            v.wait_ge(act_ssq, TC + 2 * SEG)
            link(v.tensor_reduce(stat[:, 0:2], ssp[:, :, :], AX, ALU.add))
            v.tensor_scalar(stat[:, 2:4], stat[:, 0:2], 1.0 / D, RMS_EPS, ALU.mult, ALU.add).then_inc(dve_var, 1)
            v.wait_ge(act_std, 2)
            v.reciprocal(stat[:, 6:8], stat[:, 4:6]).then_inc(dve_rstd2, 1)
            v.wait_ge(dve_rstd2, 1)

            def hn_low(tc, half):
                cols = slice(half * D // 2, (half + 1) * D // 2)
                v.wait_ge(act_hn, tc + 1)
                v.scalar_tensor_tensor(out=hn_lo[:, tc, cols], in0=hg[:, tc, cols], scalar=stat[:, 6 + tc:7 + tc],
                                       in1=hn_hi[:, tc, cols].bitcast(F32), op0=ALU.mult, op1=ALU.subtract
                                       ).then_inc(dve_hn, 1)

            def col(k):
                return stat[:, k:k + TC].rearrange("p (t a) -> p t a", a=1)

            v.wait_ge(pe_logit, 1)
            for tc in range(TC):
                last = step(v.scalar_tensor_tensor(out=logit[:, tc, :], in0=ps[:, 2 + tc, 0:NG + NE],
                                                   scalar=stat[:, 6 + tc:7 + tc], in1=brt[:, :],
                                                   op0=ALU.mult, op1=ALU.add))
            v.wait_ge(dve_step, last)
            gl = logit[:, :, 0:NG]
            el = logit[:, :, NG:NG + NE]

            def first_of(dst, src, top, width, tmp):
                link(v.tensor_tensor(rt[:, tmp, :, 0:width], src, bcast(top, 2, width), ALU.is_equal))
                d = bcast(desc[:, 0:width].rearrange("p (a w) -> p a w", a=1), 1, TC)
                link(v.tensor_tensor(rt[:, tmp, :, 0:width], rt[:, tmp, :, 0:width], d, ALU.mult))
                link(v.tensor_reduce(stat[:, 14:16], rt[:, tmp, :, 0:width], AX, ALU.max))
                link(v.tensor_tensor(dst, rt[:, tmp, :, 0:width], bcast(col(14), 2, width), ALU.is_equal))

            link(v.tensor_reduce(stat[:, 12:14], gl, AX, ALU.max))
            v.tensor_tensor(rt[:, 0, :, 0:NG], gl, bcast(col(12), 2, NG), ALU.subtract).then_inc(dve_route, 1)
            first_of(rt[:, 2, :, 0:NG], gl, col(12), NG, 3)
            link(v.tensor_scalar(rt[:, 3, :, 0:NG], rt[:, 2, :, 0:NG], -1.0, 1e30, ALU.add, ALU.mult))
            e4 = rt[:, 4, :, :].rearrange("p t (g e) -> p (t g) e", g=NG)
            for tc in range(TC):
                drop = bcast(rt[:, 3, tc, 0:NG].rearrange("p (g a) -> p g a", a=1), 2, PER_GROUP)
                last = step(v.tensor_tensor(rt[:, 4, tc, :].rearrange("p (g e) -> p g e", g=NG),
                                            logit[:, tc, NG:].rearrange("p (g e) -> p g e", g=NG),
                                            drop, ALU.add))
            v.wait_ge(dve_step, last)
            link(v.tensor_reduce(stat[:, 12:14], rt[:, 4, :, :], AX, ALU.max))
            first_of(rt[:, 5, :, :], rt[:, 4, :, :], col(12), NE, 6)
            link(v.scalar_tensor_tensor(out=rt[:, 7, :, :], in0=rt[:, 5, :, :], scalar=-2e30,
                                        in1=rt[:, 4, :, :], op0=ALU.mult, op1=ALU.add))
            link(v.tensor_reduce(stat[:, 10:12], rt[:, 7, :, :], AX, ALU.max))
            v.tensor_tensor(stat[:, 8:10], stat[:, 10:12], stat[:, 12:14], ALU.subtract).then_inc(dve_route, 1)
            first_of(rt[:, 8, :, :], rt[:, 7, :, :], col(10), NE, 6)
            v.tensor_tensor(mask[:, :, :], rt[:, 5, :, :], rt[:, 8, :, :], ALU.add).then_inc(dve_mask, 1)
            hn_low(0, 0)
            v.wait_ge(pe_rank, 1)
            for tc in range(TC):
                last = step(v.scalar_tensor_tensor(out=rank[:, tc, 0:NE], in0=ps[:, 6, NE * tc:NE * (tc + 1)],
                                                   scalar=1.0, in1=mask[:, tc, :], op0=ALU.add, op1=ALU.mult))
            v.wait_ge(dve_step, last)
            v.tensor_scalar(rank[:, :, NE:], rank[:, :, 0:QUAD], -float(SLOTS), None, ALU.add
                            ).then_inc(dve_rank, 1)
            def fill_sel(q):
                for tc in range(TC):
                    ins = v.tensor_tensor(
                        sel[:, tc, :].rearrange("p (e s) -> p e s", s=SLOTS),
                        bcast(rank[:, tc, q].rearrange("p (e a) -> p e a", a=1), 2, SLOTS),
                        bcast(iota_s[:, :].rearrange("p (a s) -> p a s", a=1), 1, QUAD), ALU.is_equal)
                return ins

            v.wait_ge(dve_rank, 1)
            fill_sel(slice(0, QUAD)).then_inc(dve_sel, 1)
            link(v.tensor_reduce(stat[:, 12:13], ps[:, 6, 2 * NE:3 * NE], AX, ALU.max))
            link(v.tensor_scalar(stat[:, 13:14], stat[:, 12:13], float(SLOTS), 1.0, ALU.is_gt, ALU.add))
            for k in range(2, T // SLOTS):
                link(v.scalar_tensor_tensor(out=stat[:, 13:14], in0=stat[:, 12:13], scalar=float(k * SLOTS),
                                            in1=stat[:, 13:14], op0=ALU.is_gt, op1=ALU.add))
            v.tensor_copy(rounds[:, :], stat[:, 13:14]).then_inc(rounds_ready, 1)
            hn_low(1, 0)
            v.wait_ge(pe_rankT, 1)
            v.tensor_copy(rankT[:, :], ps[0:NE, 7, 0:T]).then_inc(dve_rankT, 1)
            hn_low(0, 1)
            hn_low(1, 1)
            v.wait_ge(act_rexp, 1)
            v.wait_ge(rounds_ready, 1)
            link(v.tensor_reduce(stat[:, 12:14], rt[:, 1, :, 0:NG], AX, ALU.add))
            v.wait_ge(act_rexp, 2)
            link(v.scalar_tensor_tensor(out=stat[:, 14:16], in0=stat[:, 2:4], scalar=1.0,
                                        in1=stat[:, 12:14], op0=ALU.add, op1=ALU.mult))
            link(v.reciprocal(stat[:, 12:14], stat[:, 14:16]))
            link(v.tensor_tensor(stat[:, 14:16], stat[:, 12:14], stat[:, 2:4], ALU.mult))
            link(v.tensor_tensor(rt[:, 5, :, :], rt[:, 5, :, :], bcast(col(12), 2, NE), ALU.mult))
            link(v.tensor_tensor(rt[:, 8, :, :], rt[:, 8, :, :], bcast(col(14), 2, NE), ALU.mult))
            link(v.tensor_tensor(rt[:, 10, :, :], rt[:, 5, :, :], rt[:, 8, :, :], ALU.add))
            hi = comb_hl[:, :, :, 0:1].rearrange("p t e a -> p t (e a)")
            lo = comb_hl[:, :, :, 1:2].rearrange("p t e a -> p t (e a)")
            link(v.tensor_copy(hi, rt[:, 10, :, :]))
            v.tensor_tensor(lo, rt[:, 10, :, :], hi.bitcast(F32), ALU.subtract).then_inc(dve_comb, 1)

            v.wait_ge(rounds_ready, 1)
            n_rounds = nc.values_load(rounds[0:1, 0:1], engines=[ENG.DVE], min_val=1, max_val=4)
            own = n[0]
            v.wait_ge(dve_ws, 1)

            def weighted_lo(pair, yhis):
                v.wait_ge(act_yhi, yhis)
                v.scalar_tensor_tensor(out=y_lo[:, :], in0=ps[:, 6:8, :].rearrange("p a b -> p (a b)"),
                                       scalar=wslot[:, pair:pair + 1], in1=y_hi[:, :].bitcast(F32),
                                       op0=ALU.mult, op1=ALU.subtract).then_inc(dve_ylo, 1)

            with loop(ENG.DVE, 0, n_rounds) as r:
                with loop(ENG.DVE, 0, NQ) as q:
                    g = r * NQ + q
                    weighted_lo(1, g * 2 + 1)
                    for pair in range(2):
                        v.wait_ge(pe_ws, g * 2 + (pair + 1))
                        for j in range(2):
                            half = slice(SLOTS * j, SLOTS * (j + 1))
                            v.tensor_reduce(wslot[half, pair:pair + 1], ps[half, 6, 2 * j:2 * j + 2], AX, ALU.add
                                            ).then_inc(dve_ws, 1)
                        v.wait_ge(act_sg, g * 2 + (pair + 1))
                        v.tensor_tensor(hid[:, :], sgate[:, :], ps[:, 4, FE:2 * FE], ALU.mult).then_inc(dve_hid, 1)
                        if pair == 0:
                            v.wait_ge(pe_bc, g + 1)
                            v.tensor_scalar(selT[:, :, :].rearrange("p a t -> p (a t)"), ps[:, 5, :],
                                            slot_no[:, 0:1], None, ALU.is_equal).then_inc(dve_selT, 1)
                            v.wait_ge(dve_ws, g * 4 + 3)
                            weighted_lo(0, g * 2 + 2)
                        else:
                            fill_sel(bass.ds((q + 1) * QUAD, QUAD)).then_inc(dve_sel, 1)
                v.wait_ge(dve_sel, (r + 1) * NQ + 1)
                v.tensor_scalar(rank[:, :, :], rank[:, :, :], -float(SLOTS), None, ALU.add).then_inc(dve_step, 1)
                v.wait_ge(dve_selT, (r + 1) * NQ)
                v.tensor_scalar(slot_no[:, :], slot_no[:, :], float(SLOTS), None, ALU.add).then_inc(dve_step, 1)
                v.wait_ge(dve_step, r * 2 + (own + 2))
            v.wait_ge(dve_ws, n_rounds * (4 * NQ) + 1)
            for half in range(2):
                cols = slice(half * 512, (half + 1) * 512)
                v.wait_ge(act_yhi, n_rounds * (2 * NQ) + (half + 1))
                v.scalar_tensor_tensor(out=y_lo[:, cols], in0=ps[:, 6 + half, :], scalar=wslot[:, 1:2],
                                       in1=y_hi[:, cols].bitcast(F32), op0=ALU.mult, op1=ALU.subtract
                                       ).then_inc(dve_ylo, 1)
            for tc in range(TC):
                v.wait_ge(act_fssq, tc + 1)
                v.tensor_scalar(stat[:, 2 + tc:3 + tc], stat[:, tc:tc + 1], 1.0 / D, RMS_EPS, ALU.mult, ALU.add
                                ).then_inc(dve_fin, 1)
                v.wait_ge(act_fstd, tc + 1)
                v.reciprocal(stat[:, 6 + tc:7 + tc], stat[:, 4 + tc:5 + tc]).then_inc(dve_fin, 1)
                v.wait_ge(dve_fin, 2 * tc + 2)
                for half in range(2):
                    cols = slice(half * 512, (half + 1) * 512)
                    v.scalar_tensor_tensor(out=hres[:, tc, cols], in0=ps[:, 2 * tc + half, :],
                                           scalar=stat[:, 6 + tc:7 + tc], in1=gfin[:, cols],
                                           op0=ALU.mult, op1=ALU.mult).then_inc(dve_out, 1)

        @block.tensor
        def _(pe):
            def keep_warm(n):
                for _ in range(n):
                    pe.matmul(ps[:, 5, 0:P], ones[:, :], ones[:, :], start=True, stop=True)

            pe.wait_ge(gp_step, 3)
            keep_warm(7)
            for tc in range(TC):
                pe.wait_ge(x_in[tc], 16)
                for c in range(KC):
                    last = pe.transpose(ps[:, c % 4, c // 4 * T + tc * P:c // 4 * T + (tc + 1) * P],
                                        hres[:, tc, c * P:(c + 1) * P], ident[:, :])
            last.then_inc(pe_chunk, KC)
            pe.wait_ge(vec_in, 16 * 11)
            for c in range(KC):
                last = pe.transpose(ps[:, 7, c * NROW:(c + 1) * NROW], vecs[:, c * P:(c + 1) * P],
                                    ident[0:NROW, 0:NROW])
            last.then_inc(pe_par, 1)
            keep_warm(6)
            for tc in range(TC):
                pe.wait_ge(dve_rdiag, tc + 1)
                last = pe.matmul(ps[:, 6, tc * P:(tc + 1) * P], ones[:, :], rdiag[:, tc, :], start=True, stop=True)
            last.then_inc(pe_rstd, 1)
            keep_warm(7)

            def whole_panel(s, p, first=False):
                pe.wait_ge(mixw_full[p], s * 16 + 16)
                w = slot_kn(ring, MIX_SLOT + p)
                for m in (2 * p, 2 * p + 1):
                    pe.wait_ge(act_evac, s * KC + max(KC + m - 3, KC))
                    for k in range(KC):
                        if first:
                            pe.wait_ge(dve_u, k + 1)
                        last = pe.matmul(ps[:, m % 4, 0:T], w[:, k, (m % 2) * P:(m % 2 + 1) * P],
                                         actT[:, k, :], start=(k == 0), stop=(k == KC - 1))
                    last.then_inc(pe_chunk, 1)

            def split_products(dst, w_hi, w_lo, x_hi, x_lo, before=None):
                for k in range(KC):
                    if before:
                        before(k)
                    pe.matmul(dst, w_hi(k), x_hi(k), start=(k == 0), stop=False)
                    pe.matmul(dst, w_hi(k), x_lo(k), start=False, stop=False)
                    last = pe.matmul(dst, w_lo(k), x_hi(k), start=False, stop=(k == KC - 1))
                return last

            def split_panel(k, x_hi, x_lo, before):
                pe.wait_ge(dve_wlo, SPLIT.index(k) + 1)
                w_hi, w_lo = slot_kn(ring_r, HI_SLOT + k % SEG), slot_kn(ring_r, MIX_SLOT + k % SEG)
                for m in (2 * k, 2 * k + 1):
                    before(m)
                    cols = slice((m % 2) * P, (m % 2 + 1) * P)
                    split_products(ps[:, m % 4, 0:T], lambda c: w_hi[:, c, cols], lambda c: w_lo[:, c, cols],
                                   lambda c: x_hi[:, c, 0:T], lambda c: x_lo[:, c, 0:T]).then_inc(pe_chunk, 1)

            def evac_bank(m):
                pe.wait_ge(act_evac, KC + max(m - 3, 0))

            whole_panel(0, 0, first=True)
            pe.wait_ge(dve_split, 1)
            for k in SPLIT[:3]:
                split_panel(k, u_hi, u_lo, evac_bank)
            with loop(ENG.PE, 1, K_GA // SEG) as s:
                for p in range(SEG):
                    whole_panel(s, p)
            def recurrence_gates():
                pe.wait_ge(lruw_in, 32)
                for m in range(2 * KC):
                    c, w = m // 2, m % 2
                    if w == 0:
                        pe.wait_ge(dve_conv4, c + 1)
                    if m >= 4:
                        pe.wait_ge(act_lru, m - 3)
                    pe.matmul(ps[:, 4 + m % 4, 0:T], lruw[:, w, c, :], bufB[:, c, :], start=True, stop=True
                              ).then_inc(pe_lru, 1)

            def channel_sums(src, bank):
                for c in range(KC):
                    last = pe.matmul(ps[:, bank, 0:T], ones[:, :], src[:, c, :], start=(c == 0), stop=(c == KC - 1))
                last.then_inc(pe_sum, 1)

            for k in range(K_GA, K_YA):
                split_panel(k, u_hi, u_lo, evac_bank)
                if k == K_GA:
                    recurrence_gates()
                if k == K_GB:
                    pe.wait_ge(dve_conv, KC)
                    channel_sums(cpad[:, :, CONVW - 1:], 4)
                if k == K_YA - 1:
                    pe.wait_ge(act_sq, 1)
                    channel_sums(bufB, 5)
            pe.wait_ge(dve_split, 2)
            for k in range(K_YA, K_YB):
                split_panel(k, bufA_r, bufG_r, evac_bank)
            pe.wait_ge(dve_split, 4)

            def yb_bank(m):
                m -= 2 * K_YB
                if m < 4:
                    pe.wait_ge(act_evac, 8 * KC + m - 3)
                else:
                    pe.wait_ge(dve_yb, 2 * (m - 3) - 1)
            for k in range(K_YB, K_WOUT):
                split_panel(k, cpad_r, bufC_r, yb_bank)

            def h_transposes(p):
                for c in (2 * p, 2 * p + 1):
                    if c >= 2:
                        pe.wait_ge(act_hT, c - 1)
                    for tc in range(TC):
                        pe.wait_ge(dve_h, 2 * p + tc + 1)
                        last = pe.transpose(ps[:, c % 2, tc * P:(tc + 1) * P], hres[:, tc, c * P:(c + 1) * P],
                                            ident[:, :])
                    last.then_inc(pe_hT, 1)

            def logits(p):
                for c in (2 * p, 2 * p + 1):
                    pe.wait_ge(act_hT, c + 1)
                    for tc in range(TC):
                        last = pe.matmul(ps[:, 2 + tc, 0:NG + NE], actT[:, c, tc * P:(tc + 1) * P], wrt[:, c, :],
                                         start=(c == 0), stop=(c == KC - 1))
                return last

            for p in range(SEG):
                pe.wait_ge(dve_wlo, SPLIT.index(K_WOUT + p) + 1)
                w_hi, w_lo = slot_kn(ring_r, HI_SLOT + p), slot_kn(ring_r, MIX_SLOT + p)
                for tc in range(TC):
                    if p:
                        pe.wait_ge(dve_h, 2 * (p - 1) + tc + 1)
                    tok = slice(tc * P, (tc + 1) * P)
                    split_products(ps[:, 4 + tc, 0:PN], lambda k: bufA_r[:, k, tok], lambda k: gateA_r[:, k, tok],
                                   lambda k: w_hi[:, k, :], lambda k: w_lo[:, k, :],
                                   before=(lambda k: pe.wait_ge(dve_split, 4 + k + 1)) if p == tc == 0 else None
                                   ).then_inc(pe_wout, 1)
                if p >= 1:
                    h_transposes(p - 1)
                if p == 2:
                    pe.wait_ge(dve_gw, KC)
                if p >= 2:
                    logits(p - 2)
            h_transposes(SEG - 1)
            logits(SEG - 2)
            logits(SEG - 1).then_inc(pe_logit, 1)
            pe.wait_ge(gp_step, 14)
            for b in (6, 7):
                last = pe.matmul(ps[:, b, :], selT[:, 0, 0:P], selT[:, :, :].rearrange("p a t -> p (a t)"),
                                 start=True, stop=True, skip_group_check=True)
            last.then_inc(pe_down, 1)
            for b in range(4):
                if b == 0:
                    pe.wait_ge(act_hT, KC)
                if b == 2:
                    pe.wait_ge(dve_route, 1)
                last = pe.matmul(ps[:, b, :], ident[:, :], hres[:, b // 2, b % 2 * 512:(b % 2 + 1) * 512],
                                 start=True, stop=False, skip_group_check=True)
            last.then_inc(pe_h_in, 1)
            keep_warm(5)
            pe.wait_ge(dve_mask, 1)
            pe.matmul(ps[:, 6, 0:NE], tri_b[:, :], mask[:, 0, :], start=True, stop=True)
            pe.matmul(ps[:, 6, NE:2 * NE], ones_b[:, :], mask[:, 0, :], start=True, stop=False)
            pe.matmul(ps[:, 6, NE:2 * NE], tri_b[:, :], mask[:, 1, :], start=False, stop=True)
            pe.matmul(ps[:, 6, 2 * NE:3 * NE], ones_b[:, :], mask[:, 0, :], start=True, stop=False)
            pe.matmul(ps[:, 6, 2 * NE:3 * NE], ones_b[:, :], mask[:, 1, :], start=False, stop=True
                      ).then_inc(pe_rank, 1)
            pe.wait_ge(dve_rank, 1)
            for tc in range(TC):
                last = pe.transpose(ps[0:NE, 7, tc * P:(tc + 1) * P], rank[:, tc, 0:NE], ident[:, :])
            last.then_inc(pe_rankT, 1)
            keep_warm(8)

            def scatter(pair, y, halves=(0, 1), stop=False):
                for nn in halves:
                    for tc in range(TC):
                        last = pe.matmul(ps[:, 2 * tc + nn, :], selT[:, pair, tc * P:(tc + 1) * P],
                                         y[:, nn * 512:(nn + 1) * 512], start=False, stop=stop,
                                         skip_group_check=True)
                last.then_inc(pe_scat, 1)

            pe.wait_ge(dve_hn, TC)
            pe.wait_ge(rounds_ready, 1)
            n_rounds = nc.values_load(rounds[0:1, 0:1], engines=[ENG.PE], min_val=1, max_val=4)

            def mixture_step(i, u):
                g = i * SPAN + u
                q = g % NQ

                def wait_unit(n):
                    n += u * UNITS
                    if n == EXTRA:
                        pe.wait_ge(extra_full, i * 64 + 64)
                        return extra
                    loads = SPAN_UNITS // RING - (n % RING == EXTRA % RING)
                    pe.wait_ge(ex_full[n % RING], i * (64 * loads) + 64 * (n // RING + 1))
                    return unit(n % RING)

                pe.wait_ge(dve_sel, g + 1)
                for c in range(KC):
                    if c >= 4 and c % 2 == 0:
                        pe.wait_ge(act_xslot, g * (KC // 2) + (c // 2 - 1))
                    if c == KC // 2:
                        pe.wait_ge(dve_hn, 2 * TC)
                    for t, (part, tc) in enumerate([(a, b) for a in (hn_hi, hn_lo) for b in range(TC)]):
                        last = pe.matmul(ps[:, 4 + c // 2 % 2, c % 2 * T:(c % 2 + 1) * T], part[:, tc, c * P:(c + 1) * P],
                                         sel[:, tc, :], start=(t == 0), stop=(t == 2 * TC - 1))
                    if c % 2:
                        last.then_inc(pe_gather, 1)
                for pair in range(2):
                    if pair == 1:
                        pe.wait_ge(act_hidT, g * 2 + 1)
                    for k in range(KC):
                        if pair == 0 and k in (0, KC - 2):
                            pe.wait_ge(act_xslot, g * (KC // 2) + KC // 2 - (k == 0))
                        if k % (KC // 2) == 0:
                            gate_up = wait_unit(3 * pair + k // (KC // 2)).rearrange("p a (k n) -> p (a k) n", n=4 * FE)
                        for j in range(2):
                            e = 2 * pair + j
                            w = gate_up[:, k % (KC // 2), j * 2 * FE:(j + 1) * 2 * FE]
                            last = pe.matmul(ps[SLOTS * j:SLOTS * (j + 1), 4, :],
                                             xslot[:, k, e * SLOTS:(e + 1) * SLOTS], w,
                                             start=(k == 0), stop=(k == KC - 1), skip_group_check=True)
                        if k % (KC // 2) == KC // 2 - 1:
                            last.then_inc((pe_gu_half, pe_gu)[k // (KC // 2)], 1)
                    if pair == 0:
                        pe.wait_ge(dve_comb, 1)
                    pe.wait_ge(dve_ylo, g * 2 + (pair + 1))
                    for tc in range(TC):
                        last = pe.matmul(ps[:, 6, 0:4], sel[:, tc, pair * P:(pair + 1) * P],
                                         comb_hl[:, tc, bass.ds(q * QUAD + 2 * pair, 2), :].rearrange("p a b -> p (a b)"),
                                         start=(tc == 0), stop=(tc == TC - 1))
                    last.then_inc(pe_ws, 1)
                    if pair == 1:
                        pe.wait_ge(dve_selT, g + 1)
                    scatter(1 - pair, y_hi)
                    pe.wait_ge(dve_hid, g * 2 + (pair + 1))
                    for f in range(FC):
                        last = pe.transpose(ps[:, 4, f * P:(f + 1) * P], hid[:, f * P:(f + 1) * P], ident[:, :])
                    last.then_inc(pe_hidT, 1)
                    scatter(1 - pair, y_lo)
                    if pair == 0:
                        pe.wait_ge(rankq_in, 16 * NQ)
                        for a in range(2):
                            last = pe.matmul(ps[:, 5, a * T:(a + 1) * T], pair_row[:, a, :],
                                             rank_q[:, bass.ds(q, 1), :].rearrange("e a t -> e (a t)"),
                                             start=True, stop=True)
                        last.then_inc(pe_bc, 1)
                    down = wait_unit(3 * pair + 2)
                    pe.wait_ge(act_hidT, g * 2 + (pair + 1))
                    pe.wait_ge(dve_ws, g * 4 + (2 * pair + 3))
                    for nn in range(2):
                        for f in range(FC):
                            for j in range(2):
                                w = down[:, j, :].rearrange("p (f n) -> p f n", f=FC)
                                last = pe.matmul(ps[SLOTS * j:SLOTS * (j + 1), 6 + nn, :],
                                                 hidT[:, f, SLOTS * j:SLOTS * (j + 1)],
                                                 w[:, f, nn * 512:(nn + 1) * 512],
                                                 start=(f == 0), stop=(f == FC - 1), skip_group_check=True)
                        last.then_inc((pe_down_half, pe_down)[nn], 1)

            with loop(ENG.PE, 0, n_rounds * (NQ // SPAN)) as i:
                for u in range(SPAN):
                    mixture_step(i, u)
            for half in range(2):
                pe.wait_ge(act_yhi, n_rounds * (2 * NQ) + (half + 1))
                scatter(1, y_hi, halves=(half,))
            for half in range(2):
                pe.wait_ge(dve_ylo, n_rounds * (2 * NQ) + (half + 1))
                scatter(1, y_lo, halves=(half,), stop=True)


_INS = ["x", "g_mix", "w_in", "rnn_conv_w", "rnn_conv_b", "lru_w_r", "lru_b_r", "lru_w_i", "lru_b_i",
        "lru_a_param", "w_rnn_out", "conf_conv_w", "conf_conv_b", "conf_ln_g", "conf_ln_b", "w_conf_out",
        "w_out", "g_ffn", "w_group_router", "b_group_router", "w_expert_router", "b_expert_router",
        "w_gate", "w_up", "w_down", "g_final"]


def kernel(**inputs):
    import numpy as np
    import concourse.bacc as bacc
    from concourse.bass_utils import run_bass_kernel_spmd

    nc = bacc.Bacc("TRN2", target_bir_lowering=False, num_devices=1)
    arrays, args = {}, []
    for name in _INS:
        a = np.ascontiguousarray(inputs[name])
        arrays[f"in_{name}"] = a
        args.append(nc.dram_tensor(f"in_{name}", a.shape, mybir.dt.from_np(a.dtype), kind="ExternalInput").ap())
    shape = inputs["x"].shape
    out = nc.dram_tensor("out", shape, F32, kind="ExternalOutput").ap()
    build(nc, *args, out)
    r = run_bass_kernel_spmd(nc, [arrays], core_ids=[0])
    return r.results[0]["out"]
```
